# Optimizing a Trainium2 kernel written in Bass

```python
import jax, jax.numpy as jnp
from jax import lax
import numpy as np

D_MODEL = 1024
BATCH = 1
SEQ = 1024
DEPTH = 1

CHUNK = 64
D_MIX = D_MODEL
ATTN_WIDTH = D_MIX // 2
HGRN_WIDTH = D_MIX - ATTN_WIDTH
ATTN_HEAD_DIM = 64
ATTN_HEADS = ATTN_WIDTH // ATTN_HEAD_DIM
HGRN_HEAD_DIM = 128
HGRN_HEADS = HGRN_WIDTH // HGRN_HEAD_DIM
LEFT_CHUNKS = 8
BAND = (LEFT_CHUNKS + 1) * CHUNK
REL_CLIP = 128
N_REL = 2 * REL_CLIP + 1
D_FF = 2816
RMS_EPS = 1e-6
PROJ_SIZES = (ATTN_WIDTH, ATTN_WIDTH, ATTN_WIDTH, HGRN_WIDTH, HGRN_WIDTH, HGRN_WIDTH, HGRN_WIDTH)
PROJ_COLS = sum(PROJ_SIZES)
PROJ_SPLITS = tuple(int(v) for v in np.cumsum(PROJ_SIZES)[:-1])

kernel_name = "hybrid_chunk_attn_hgrn2_macaron"

def rms_norm(x, g):
    xf = x.astype(jnp.float32)
    y = xf * lax.rsqrt(jnp.mean(xf * xf, axis=-1, keepdims=True) + RMS_EPS)
    return (y * g.astype(jnp.float32)).astype(x.dtype)

def swiglu_ffn(h, w_gate, w_up, w_down):
    return (jax.nn.silu(h @ w_gate) * (h @ w_up)) @ w_down

def chunked_band_attention(q, k, v, rel_bias):
    B, S, H, Dh = q.shape
    n_chunks = S // CHUNK
    pad = LEFT_CHUNKS * CHUNK
    k_pad = jnp.pad(k, ((0, 0), (pad, 0), (0, 0), (0, 0)))
    v_pad = jnp.pad(v, ((0, 0), (pad, 0), (0, 0), (0, 0)))
    t_pos = jnp.arange(CHUNK)[:, None] + pad
    s_pos = jnp.arange(BAND)[None, :]
    rel_idx = jnp.clip(t_pos - s_pos, -REL_CLIP, REL_CLIP) + REL_CLIP
    bias = rel_bias.astype(jnp.float32)[:, rel_idx]
    scale = Dh ** -0.5
    q_chunks = q.reshape(B, n_chunks, CHUNK, H, Dh).transpose(1, 0, 2, 3, 4)

    def one_chunk(args):
        c, qc = args
        start = c * CHUNK
        kb = lax.dynamic_slice_in_dim(k_pad, start, BAND, axis=1)
        vb = lax.dynamic_slice_in_dim(v_pad, start, BAND, axis=1)
        scores = jnp.einsum('bqhd,bkhd->bhqk', qc, kb,
                            preferred_element_type=jnp.float32) * scale + bias
        key_pos = start - pad + jnp.arange(BAND)
        scores = jnp.where((key_pos >= 0)[None, None, None, :], scores, -jnp.inf)
        p = jax.nn.softmax(scores, axis=-1)
        return jnp.einsum('bhqk,bkhd->bqhd', p.astype(vb.dtype), vb)

    out = lax.map(one_chunk, (jnp.arange(n_chunks), q_chunks))
    return out.transpose(1, 0, 2, 3, 4).reshape(B, S, H * Dh)

def hgrn2_chunkwise(q, k, v, log_f):
    B, S, H, Dk = q.shape
    Dv = v.shape[-1]
    n_chunks = S // CHUNK

    def to_chunks(a):
        return a.reshape(B, n_chunks, CHUNK, H, a.shape[-1]).transpose(1, 0, 3, 2, 4)

    qc, kc, vc, gc = to_chunks(q), to_chunks(k), to_chunks(v), to_chunks(log_f)
    causal = jnp.tril(jnp.ones((CHUNK, CHUNK), dtype=bool))[None, None, :, :, None]

    def step(state, inp):
        qi, ki, vi, gi = inp
        b = jnp.cumsum(gi, axis=2)
        diff = b[:, :, :, None, :] - b[:, :, None, :, :]
        decay = jnp.exp(jnp.where(causal, diff, -jnp.inf))
        scores = jnp.einsum('bhtk,bhsk,bhtsk->bhts', qi, ki, decay)
        o = (jnp.einsum('bhts,bhsv->bhtv', scores, vi)
             + jnp.einsum('bhtk,bhkv->bhtv', qi * jnp.exp(b), state))
        b_last = b[:, :, -1:, :]
        new_state = (state * jnp.exp(b_last[:, :, 0, :])[..., None]
                     + jnp.einsum('bhsk,bhsv->bhkv', ki * jnp.exp(b_last - b), vi))
        return new_state, o

    s0 = jnp.zeros((B, H, Dk, Dv), jnp.float32)
    _, o = lax.scan(step, s0, (qc, kc, vc, gc))
    return o.transpose(1, 0, 3, 2, 4).reshape(B, S, H, Dv)

def setup_inputs(seed: int = 0) -> dict:
    key = jax.random.key(seed)
    ks = jax.random.split(key, 20)
    f32 = jnp.float32

    def w(k, shape, fan_in):
        return jax.random.normal(k, shape, f32) * (fan_in ** -0.5)

    def gain(k, shape):
        return 1.0 + 0.05 * jax.random.normal(k, shape, f32)

    return {
        "x": jax.random.normal(ks[0], (BATCH, SEQ, D_MODEL), f32),
        "ffn1_norm_g": gain(ks[1], (DEPTH, D_MODEL)),
        "ffn1_w_gate": w(ks[2], (DEPTH, D_MODEL, D_FF), D_MODEL),
        "ffn1_w_up": w(ks[3], (DEPTH, D_MODEL, D_FF), D_MODEL),
        "ffn1_w_down": w(ks[4], (DEPTH, D_FF, D_MODEL), D_FF),
        "mix_norm_g": gain(ks[5], (DEPTH, D_MODEL)),
        "w_in": w(ks[6], (DEPTH, D_MODEL, PROJ_COLS), D_MODEL),
        "attn_q_norm_g": gain(ks[7], (DEPTH, ATTN_HEAD_DIM)),
        "attn_k_norm_g": gain(ks[8], (DEPTH, ATTN_HEAD_DIM)),
        "attn_rel_bias": 0.1 * jax.random.normal(ks[9], (DEPTH, ATTN_HEADS, N_REL), f32),
        "hgrn_lower_bounds": 0.1 * jax.random.normal(ks[10], (DEPTH + 1, HGRN_WIDTH), f32),
        "hgrn_out_norm_g": gain(ks[11], (DEPTH, HGRN_HEAD_DIM)),
        "w_out": w(ks[12], (DEPTH, D_MIX, D_MODEL), D_MIX),
        "ffn2_norm_g": gain(ks[13], (DEPTH, D_MODEL)),
        "ffn2_w_gate": w(ks[14], (DEPTH, D_MODEL, D_FF), D_MODEL),
        "ffn2_w_up": w(ks[15], (DEPTH, D_MODEL, D_FF), D_MODEL),
        "ffn2_w_down": w(ks[16], (DEPTH, D_FF, D_MODEL), D_FF),
    }

def reference(x, ffn1_norm_g, ffn1_w_gate, ffn1_w_up, ffn1_w_down, mix_norm_g, w_in,
              attn_q_norm_g, attn_k_norm_g, attn_rel_bias, hgrn_lower_bounds, hgrn_out_norm_g,
              w_out, ffn2_norm_g, ffn2_w_gate, ffn2_w_up, ffn2_w_down):
    B, S, _ = x.shape
    lb_all = jnp.cumsum(jax.nn.softmax(hgrn_lower_bounds.astype(jnp.float32), axis=0), axis=0)

    for l in range(DEPTH):
        h = rms_norm(x, ffn1_norm_g[l])
        x = x + 0.5 * swiglu_ffn(h, ffn1_w_gate[l], ffn1_w_up[l], ffn1_w_down[l])

        h = rms_norm(x, mix_norm_g[l])
        proj = h @ w_in[l]
        aq, ak, av, hq, hf, hi, hg = jnp.split(proj, PROJ_SPLITS, axis=-1)

        aq = rms_norm(aq.reshape(B, S, ATTN_HEADS, ATTN_HEAD_DIM), attn_q_norm_g[l])
        ak = rms_norm(ak.reshape(B, S, ATTN_HEADS, ATTN_HEAD_DIM), attn_k_norm_g[l])
        av = av.reshape(B, S, ATTN_HEADS, ATTN_HEAD_DIM)
        attn_out = chunked_band_attention(aq, ak, av, attn_rel_bias[l])

        lb = lb_all[l]
        f = lb + (1.0 - lb) * jax.nn.sigmoid(hf.astype(jnp.float32))
        shp = (B, S, HGRN_HEADS, HGRN_HEAD_DIM)
        rq = jax.nn.silu(hq.astype(jnp.float32)).reshape(shp)
        rk = (1.0 - f).reshape(shp)
        rv = hi.astype(jnp.float32).reshape(shp)
        ro = hgrn2_chunkwise(rq, rk, rv, jnp.log(f).reshape(shp))
        ro = rms_norm(ro, hgrn_out_norm_g[l]) * jax.nn.silu(hg.astype(jnp.float32).reshape(shp))
        hgrn_out = ro.reshape(B, S, HGRN_WIDTH).astype(x.dtype)

        x = x + jnp.concatenate([attn_out, hgrn_out], axis=-1) @ w_out[l]

        h = rms_norm(x, ffn2_norm_g[l])
        x = x + 0.5 * swiglu_ffn(h, ffn2_w_gate[l], ffn2_w_up[l], ffn2_w_down[l])
    return x


_drawn_inputs = setup_inputs


def setup_inputs(seed=0):
    import zlib

    import numpy as np

    out = dict(_drawn_inputs(seed))
    spreads = {}
    factors = {'attn_q_norm_g': 8.0,
     'attn_k_norm_g': 8.0,
     'attn_rel_bias': 8.0,
     'hgrn_lower_bounds': 8.0,
     'hgrn_out_norm_g': 2.704,
     'ffn2_norm_g': 2.968}
    for name, (base, spread) in spreads.items():
        noise = np.random.default_rng([zlib.crc32(name.encode()), seed]).standard_normal(out[name].shape)
        drawn = base * np.exp(spread * noise) if base else spread * noise
        out[name] = __import__('jax').numpy.asarray(drawn.astype(out[name].dtype))
    for name, factor in factors.items():
        out[name] = (out[name] * factor).astype(out[name].dtype)
    return out
```

```python
from contextlib import ExitStack

import numpy as np

import concourse.bass as bass
from concourse import mybir

F32 = mybir.dt.float32
F32R = mybir.dt.float32r
U8 = mybir.dt.uint8
ALU = mybir.AluOpType
ACT = mybir.ActivationFunctionType
AX_X = mybir.AxisListType.X

P = 128
T = 1024
D = 1024
TT = T // P
KT = D // P
HALF = 512
D_FF = 2816
FT = D_FF // P
NG = FT // 2
AH = 8
DH = 64
AW = AH * DH
HH = 4
CHUNK = 64
KEY_TILES = 5
BAND = KEY_TILES * P
N_REL = 257
REL_CLIP = 128
EXT = 768
EPS = 1e-6
MASKED = -1.0e30

RING = 4
PIECES_FFN = 3 * FT
PIECES_MIX = 4 * 7
PIECES_OUT = 8
P_FFN1 = 0
P_MIX = P_FFN1 + PIECES_FFN
P_OUT = P_MIX + PIECES_MIX
P_FFN2 = P_OUT + PIECES_OUT

ADDS_FFN = NG * 16
A_FFN1 = 0
A_OUT = A_FFN1 + ADDS_FFN
A_FFN2 = A_OUT + 16

R_FFN1, R_MIX, R_CAT, R_FFN2 = range(4)

LEVEL_AT = {1: 0, 2: 1, 4: 2, 5: 3, 7: 4, 8: 5, 10: 6, 11: 7}
TURN_AT, OUTER_AT, READ_AT = 13, 14, 15
LEVELS = 8


def level_masks():
    m = np.zeros((P, LEVELS - 1, P // 2), np.float32)
    for level in range(1, LEVELS):
        h = 1 << (level - 1)
        for b in range(P // (2 * h)):
            m[2 * h * b:2 * h * b + h, level - 1, b * h:(b + 1) * h] = 1
    return m.reshape(P, -1)


def build(nc, x, ffn1_norm_g, ffn1_w_gate, ffn1_w_up, ffn1_w_down, mix_norm_g, w_in, attn_q_norm_g,
          attn_k_norm_g, attn_rel_bias, hgrn_lower_bounds, hgrn_out_norm_g, w_out, ffn2_norm_g,
          ffn2_w_gate, ffn2_w_up, ffn2_w_down, identity, masks, out):
    ds = bass.DynSlice
    with ExitStack() as ctx:
        feat = nc.dram_tensor("feat_scratch", [2 * HH * P, T], F32, kind="Internal").ap()
        tok = nc.dram_tensor("tok_scratch", [T, 5, HALF], F32, kind="Internal").ap()
        ro_d = nc.dram_tensor("ro_scratch", [T, HALF], F32, kind="Internal").ap()
        bias_d = nc.dram_tensor("bias_scratch", [AH, P, BAND], F32, kind="Internal").ap()
        ext_d = nc.dram_tensor("ext_scratch", [AH, EXT], F32, kind="Internal").ap()

        def keep(name, shape, dt=F32, where=ctx, side="left"):
            return where.enter_context(nc.sbuf_tensor(name, shape, dt, side=side))

        def sem(name):
            return ctx.enter_context(nc.semaphore(name))

        xs = keep("xs", [P, TT, D])
        raw = keep("raw", [P, RING, 1024])
        whi = keep("whi", [P, RING, 1024], F32R)
        wlo = keep("wlo", [P, RING, 1024], F32R)
        y = keep("y", [P, 2, D])
        junk = keep("junk", [P, 1024])
        gain = keep("gain", [P, D])
        ident = keep("ident", [P, P])
        ss = keep("ss", [P, 3 * TT])
        rstd = keep("rstd", [P, 3 * TT])
        mhalf = keep("mhalf", [P, 16])
        lbs = keep("lbs", [P, 2, HH])
        lb = keep("lb", [P, 3, HH])
        gn = keep("gn", [P, P])
        qkg = keep("qkg", [P, 2])

        with ExitStack() as c:
            hThi = keep("hThi", [P, KT, T], F32R, c)
            hTlo = keep("hTlo", [P, KT, T], F32R, c)
        with ExitStack() as c:
            qin = keep("q_in", [P, TT, P], where=c)
            kin = keep("k_in", [P, TT, P], where=c)
            vin = keep("v_in", [P, TT, P], where=c)
            qT = keep("qT", [P, T], where=c)
            kT = keep("kT", [P, T], where=c)
            bias = keep("bias", [P, 2, BAND], where=c)
            S = keep("S", [P, 2, BAND], where=c)
            Pr = keep("Pr", [P, 2, BAND], where=c)
            PT = keep("PT", [P, 2, BAND], where=c)
            relrow = keep("relrow", [AH, N_REL], where=c)
            extrow = keep("extrow", [AH, EXT], where=c)
            ssq = keep("ssq", [P, 2, 16], where=c)
            rsq = keep("rsq", [P, 2, 16], where=c)
            nmax = keep("nmax", [P, 2, TT], where=c)
            psumr = keep("psumr", [P, 2, TT], where=c)
            rcp = keep("rcp", [P, 2, TT], where=c)
        with ExitStack() as c:
            hidhi = keep("hidhi", [P, 2, 2, T], F32R, c, "right")
            hidlo = keep("hidlo", [P, 2, 2, T], F32R, c, "right")
            sil = keep("sil", [P, 2, HALF], where=c, side="right")
            prod = keep("prod", [P, 2, HALF], where=c, side="right")
        with ExitStack() as c:
            fF = keep("fF", [P, T], where=c, side="right")
            fQ = keep("fQ", [P, T], where=c, side="right")
            hK = keep("hK", [P, T], where=c, side="right")
            hQ = keep("hQ", [P, T], where=c, side="right")
            hV = keep("hV", [P, TT, P], where=c, side="right")
            hG = keep("hG", [P, TT, P], where=c, side="right")
            tot = keep("tot", [P, T], where=c, side="right")
            aT = keep("aT", [P, T], where=c, side="right")
            kS = keep("kS", [P, TT, P], where=c, side="right")
            st = keep("st", [P, TT, P], where=c, side="right")
            mk = keep("mk", [P, (LEVELS - 1) * HALF], U8, c, "right")
            sso = keep("sso", [P, TT], where=c, side="right")
            rso = keep("rso", [P, TT], where=c, side="right")
        with ExitStack() as c:
            cat = keep("cat", [P, TT, D], where=c, side="right")

        ps = ctx.enter_context(nc.psum_tensor("ps", [P, 8 * HALF], F32))

        def bank(b, n=HALF):
            return ps[:, b * HALF:b * HALF + n]

        x_loaded = [sem(f"x_loaded{t}") for t in range(TT)]
        ident_loaded = sem("ident_loaded")
        lb_loaded = sem("lb_loaded")
        gn_loaded = sem("gn_loaded")
        gain_loaded = sem("gain_loaded")
        mhalf_set = sem("mhalf_set")
        raw_loaded = [sem(f"raw_loaded{s}") for s in range(RING)]
        split_hi = sem("split_hi")
        split_lo = sem("split_lo")
        piece_used = sem("piece_used")
        ss_ready = sem("ss_ready")
        var_ready = sem("var_ready")
        rstd_ready = sem("rstd_ready")
        y_ready = sem("y_ready")
        turned = sem("turned")
        hT_hi_ready = sem("hT_hi_ready")
        hT_ready = sem("hT_ready")
        gate_done = sem("gate_done")
        up_done = sem("up_done")
        silu_done = sem("silu_done")
        prod_done = sem("prod_done")
        hid_hi_ready = sem("hid_hi_ready")
        hid_ready = sem("hid_ready")
        row_done = sem("row_done")
        x_added = sem("x_added")
        out_stored = sem("out_stored")
        proj_done = sem("proj_done")
        proj_evac = sem("proj_evac")
        proj_stored = [sem(f"proj_stored{s}") for s in range(4)]
        lb_diff = sem("lb_diff")
        lb_sig = sem("lb_sig")
        lb_ready = sem("lb_ready")
        sig_ready = sem("sig_ready")
        mask_loaded = sem("mask_loaded")
        mask_set = sem("mask_set")
        fq_loaded = sem("fq_loaded")
        v_loaded = sem("v_loaded")
        g_loaded = sem("g_loaded")
        hgrn_step = sem("hgrn_step")
        scaled = sem("scaled")
        scores_done = sem("scores_done")
        scores_kept = sem("scores_kept")
        k_turned = sem("k_turned")
        k_rows = sem("k_rows")
        outer_done = sem("outer_done")
        state_step = sem("state_step")
        read_done = sem("read_done")
        read_sq = sem("read_sq")
        read_ss = sem("read_ss")
        read_var = sem("read_var")
        read_rstd = sem("read_rstd")
        gate_gained = sem("gate_gained")
        ro_ready = sem("ro_ready")
        ro_stored = sem("ro_stored")
        rel_loaded = sem("rel_loaded")
        ext_step = sem("ext_step")
        ext_stored = sem("ext_stored")
        bias_stored = sem("bias_stored")
        qk_gain_loaded = sem("qk_gain_loaded")
        qk_gain_ready = sem("qk_gain_ready")
        qk_loaded = sem("qk_loaded")
        av_loaded = sem("av_loaded")
        bias_loaded = sem("bias_loaded")
        bias_masked = sem("bias_masked")
        qk_sq = sem("qk_sq")
        qk_ss = sem("qk_ss")
        qk_var = sem("qk_var")
        qk_rstd = sem("qk_rstd")
        qk_normed = sem("qk_normed")
        qk_turned = sem("qk_turned")
        qkT_ready = sem("qkT_ready")
        unit_scores = sem("unit_scores")
        unit_max = sem("unit_max")
        unit_exp = sem("unit_exp")
        unit_turned = sem("unit_turned")
        unit_PT = sem("unit_PT")
        unit_out = sem("unit_out")
        rcp_ready = sem("rcp_ready")
        head_out = sem("head_out")
        cat_loaded = sem("cat_loaded")
        dve_passed = sem("dve_passed")
        pool_passed = sem("pool_passed")

        block = ctx.enter_context(nc.Block())

        def norm_no(R):
            return R if R < R_CAT else 2

        @block.sync
        def _(sp):
            def piece(n0, adv, src, shape):
                if n0 >= RING:
                    sp.wait_ge(split_lo, n0 - RING + 1 + adv)
                dst = raw[:, n0 % RING, :]
                if shape:
                    dst = dst.rearrange("p (k c) -> p k c", k=shape)
                sp.dma_start(dst, src).then_inc(raw_loaded[n0 % RING], 16)

            def ffn(base, w_gate, w_up, w_down):
                wg = w_gate[0].rearrange("(k p) f -> p k f", p=P)
                wu = w_up[0].rearrange("(k p) f -> p k f", p=P)

                def gate_up(f, n0, adv):
                    piece(n0, adv, wg[:, :, ds(f * P, P)], KT)
                    piece(n0 + 1, adv, wu[:, :, ds(f * P, P)], KT)

                def down(f, n0, adv):
                    piece(n0, adv, w_down[0][ds(f * P, P), :], 0)

                gate_up(0, base, 0)
                gate_up(1, base + 2, 0)
                with sp.Fori(0, NG // 2) as i:
                    for g in range(2):
                        n0 = base + 4 + 6 * g
                        gate_up(4 * i + 2 + 2 * g, n0, 12 * i)
                        gate_up(4 * i + 3 + 2 * g, n0 + 2, 12 * i)
                        down(4 * i + 2 * g, n0 + 4, 12 * i)
                        down(4 * i + 2 * g + 1, n0 + 5, 12 * i)
                down(FT - 2, base + PIECES_FFN - 2, 0)
                down(FT - 1, base + PIECES_FFN - 1, 0)

            sp.dma_start(xs[:, 0, :], x[0, 0:P, :]).then_inc(x_loaded[0], 16)
            ffn(P_FFN1, ffn1_w_gate, ffn1_w_up, ffn1_w_down)

            wi = w_in[0].rearrange("(q k p) c -> q p k c", p=P, k=2)

            def mix_group(col, n0, adv):
                for q in range(4):
                    piece(n0 + q, adv, wi[q][:, :, ds(col, HALF)], 2)

            with sp.Fori(0, 4) as n:
                mix_group(HALF * n + 3 * HALF, P_MIX, 4 * n)
            with sp.Fori(0, 3) as n:
                mix_group(HALF * n, P_MIX + 16, 4 * n)
            wo = w_out[0].rearrange("(q k p) c -> q p k c", p=P, k=2)
            for h in range(2):
                for q in range(4):
                    piece(P_OUT + 4 * h + q, 0, wo[q][:, :, h * HALF:(h + 1) * HALF], 2)
            ffn(P_FFN2, ffn2_w_gate, ffn2_w_up, ffn2_w_down)

        @block.tensor
        def _(pe):
            def three(dst, a, b, first, last):
                (ahi, alo), (bhi, blo) = a, b
                pe.matmul(dst, ahi, bhi, start=first, stop=False)
                pe.matmul(dst, ahi, blo, start=False, stop=False)
                return pe.matmul(dst, alo, bhi, start=False, stop=last)

            def turn_tile(R, t):
                r = TT * R + t
                if R == R_CAT:
                    if t == 0:
                        pe.wait_ge(head_out, AH)
                        pe.wait_ge(cat_loaded, 16)
                    src = cat[:, t, :]
                else:
                    q = TT * norm_no(R) + t
                    pe.wait_ge(y_ready, q + 1)
                    src = y[:, t % 2, :]
                if r >= 2:
                    pe.wait_ge(hT_ready, r - 1)
                if t < 2 and R in (R_MIX,):
                    pe.wait_ge(prod_done, 2 * FT)
                for k in range(KT):
                    mm = pe.transpose(ps[:, (t % 2) * 1024 + k * P:(t % 2) * 1024 + (k + 1) * P],
                                      src[:, k * P:(k + 1) * P], ident[:, :])
                mm.then_inc(turned, 1)

            def ffn(F, base, adds, R):
                e_base = 2 * FT * F

                def gate_up(f0, advf, n0, adv):
                    for which in range(2):
                        s = (n0 + which) % RING
                        for h in range(2):
                            e = e_base + 2 * f0 + h
                            pe.wait_ge(split_lo, n0 + which + 1 + adv)
                            if f0 == 0:
                                pe.wait_ge(hT_ready, TT * R + (7 if which == h == 0 else 8))
                            elif which == 0:
                                pe.wait_ge(silu_done, e - 1 + 2 * advf)
                            else:
                                pe.wait_ge(prod_done, e - 1 + 2 * advf)
                            for k in range(KT):
                                mm = three(bank(2 * which + h),
                                           [w[:, s, k * P:(k + 1) * P] for w in (whi, wlo)],
                                           [a[:, k, h * HALF:(h + 1) * HALF] for a in (hThi, hTlo)],
                                           k == 0, k == KT - 1)
                            mm.then_inc((gate_done, up_done)[which], 1)

                def down(g0, advg, n0, adv, tail=None):
                    par = g0 % 2
                    pe.wait_ge(split_lo, n0 + 2 + adv)
                    pe.wait_ge(hid_ready, e_base + 4 * g0 + 4 + 4 * advg)
                    for t in range(TT):
                        for h in range(2):
                            d = adds + 16 * g0 + 2 * t + h
                            if d >= 4:
                                pe.wait_ge(x_added, d - 3 + 16 * advg)
                            for j in range(2):
                                s = (n0 + j) % RING
                                mm = three(bank(4 + d % 4),
                                           [a[:, par, j, t * P:(t + 1) * P] for a in (hidhi, hidlo)],
                                           [w[:, s, h * HALF:(h + 1) * HALF] for w in (whi, wlo)],
                                           j == 0, j == 1)
                            mm.then_inc(row_done, 1)
                        if tail is not None and t >= 2:
                            turn_tile(tail, t - 2)
                    if tail is not None:
                        turn_tile(tail, TT - 2)
                        turn_tile(tail, TT - 1)

                gate_up(0, 0, base, 0)
                gate_up(1, 0, base + 2, 0)
                with pe.Fori(0, NG // 2) as i:
                    for g in range(2):
                        n0 = base + 4 + 6 * g
                        gate_up(2 + 2 * g, 4 * i, n0, 12 * i)
                        gate_up(3 + 2 * g, 4 * i, n0 + 2, 12 * i)
                        down(g, 2 * i, n0 + 4, 12 * i)
                down(NG - 1, 0, base + PIECES_FFN - 2, 0, tail=R_MIX if F == 0 else None)

            pe.wait_ge(ident_loaded, 16)
            for t in range(TT):
                turn_tile(R_FFN1, t)
            ffn(0, P_FFN1, A_FFN1, R_FFN1)

            def group(n0, advn, feature, hook):
                base = P_MIX + 4 * n0
                for o in range(8):
                    idx = 8 * n0 + o
                    if idx >= 4:
                        pe.wait_ge(proj_evac, idx - 3 + 8 * advn)
                    else:
                        pe.wait_ge(x_added, A_OUT)
                    if n0 == 0:
                        pe.wait_ge(hT_ready, TT * R_MIX + 4 * (o % 2) + 4)
                    for k in range(KT):
                        s = (base + k // 2) % RING
                        if o == 0 and k % 2 == 0:
                            pe.wait_ge(split_lo, base + k // 2 + 1 + 4 * advn)
                        c0 = (k % 2) * HALF
                        if feature:
                            f, h = o // 2, o % 2
                            a = [w[:, s, c0 + f * P:c0 + (f + 1) * P] for w in (whi, wlo)]
                            b = [v[:, k, h * HALF:(h + 1) * HALF] for v in (hThi, hTlo)]
                        else:
                            a = [v[:, k, o * P:(o + 1) * P] for v in (hThi, hTlo)]
                            b = [w[:, s, c0:c0 + HALF] for w in (whi, wlo)]
                        mm = three(bank(4 + o % 4), a, b, k == 0, k == KT - 1)
                        if o == 7 and k % 2 == 1 and k < KT - 1:
                            mm.then_inc(piece_used, 1)
                        if k == 3:
                            hook(2 * o)
                    mm.then_inc(proj_done, 1)
                    hook(2 * o + 1)

            def hgrn(j):
                def hook(at):
                    if at in LEVEL_AT:
                        L = LEVEL_AT[at]
                        pe.wait_ge(scaled, 9 * j + L + 1)
                        if L == 0:
                            pe.wait_ge(ro_ready, j + 1)
                            for c in range(TT):
                                mm = pe.matmul(ps[:, c * P:(c + 1) * P], hK[:, c * P:(c + 1) * P],
                                               fQ[:, c * P:(c + 1) * P], start=True, stop=True)
                        else:
                            h = 1 << (L - 1)
                            if L >= 3:
                                pe.wait_ge(scores_kept, 8 * j + L - 1)
                            b = 2 + L % 2
                            q = hQ[:, :].rearrange("p (c b two h) -> p c b two h", c=TT, two=2, h=h)
                            for c in range(TT):
                                mm = pe.matmul(
                                    ps[:, b * HALF + c * 64:b * HALF + (c + 1) * 64],
                                    hK[:, c * P:(c + 1) * P], q[:, c, :, 1, :], start=True, stop=True)
                        mm.then_inc(scores_done, 1)
                    elif at == TURN_AT:
                        pe.wait_ge(scaled, 9 * j + 9)
                        for c in range(TT):
                            mm = pe.transpose(ps[:, c * P:(c + 1) * P], hK[:, c * P:(c + 1) * P], ident[:, :])
                        mm.then_inc(k_turned, 1)
                    elif at == OUTER_AT:
                        pe.wait_ge(k_rows, j + 1)
                        pe.wait_ge(v_loaded, 16 * j + 16)
                        pe.wait_ge(scores_kept, 8 * j + 8)
                        for c in range(TT - 1):
                            mm = pe.matmul(ps[:, 2 * HALF + c * P:2 * HALF + (c + 1) * P],
                                           kS[:, c, :], hV[:, c, :], start=True, stop=True)
                        mm.then_inc(outer_done, 1)
                    elif at == READ_AT:
                        pe.wait_ge(state_step, 7 * j + 7)
                        for c in range(TT):
                            dst = ps[:, c * P:(c + 1) * P]
                            mm = pe.matmul(dst, aT[:, c * P:(c + 1) * P], hV[:, c, :],
                                           start=True, stop=(c == 0))
                            if c:
                                mm = pe.matmul(dst, hQ[:, c * P:(c + 1) * P], st[:, c, :],
                                               start=False, stop=True)
                        mm.then_inc(read_done, 1)
                return hook

            def nothing(at):
                return None

            group(0, 0, True, nothing)
            group(1, 0, True, nothing)
            group(2, 0, False, nothing)
            pe.nop().then_inc(k_turned, 1)
            pe.nop().then_inc(read_done, 1)
            with pe.Fori(0, HH) as j:
                group(3, j, False, hgrn(j))

            def pair(i):
                for w, src in ((0, qin), (1, kin)):
                    pe.wait_ge(qk_normed, 2 * i + w + 1)
                    for t in range(TT):
                        b = (0, 2)[w]
                        mm = pe.transpose(ps[:, b * HALF + t * P:b * HALF + (t + 1) * P], src[:, t, :], ident[:, :])
                    mm.then_inc(qk_turned, 1)
                pe.wait_ge(qkT_ready, 2 * i + 2)

                def n_keys(u):
                    return min(u // 2 + 1, KEY_TILES)

                def scores(u):
                    t, hd, n = u // 2, u % 2, n_keys(u)
                    if u >= 2:
                        pe.wait_ge(unit_max, 16 * i + u - 1)
                    rows = slice(hd * DH, (hd + 1) * DH)
                    b = 2 * (u % 2) * HALF
                    lo = (t - n + 1) * P
                    m = min(n * P, HALF)
                    mm = pe.matmul(ps[:, b:b + m], qT[rows, t * P:(t + 1) * P],
                                   kT[rows, lo:lo + m], start=True, stop=True)
                    if n * P > HALF:
                        mm = pe.matmul(ps[:, b + m:b + n * P], qT[rows, t * P:(t + 1) * P],
                                       kT[rows, lo + m:lo + n * P], start=True, stop=True)
                    mm.then_inc(unit_scores, 1)

                def turn(u):
                    n = n_keys(u)
                    pe.wait_ge(unit_exp, 16 * i + u + 1)
                    if u >= 1:
                        pe.wait_ge(unit_PT, 16 * i + u)
                    for c in range(n):
                        mm = pe.transpose(ps[:, 4 * HALF + c * P:4 * HALF + (c + 1) * P],
                                          Pr[:, u % 2, c * P:(c + 1) * P], ident[:, :])
                    mm.then_inc(unit_turned, 1)

                def values(u):
                    t, hd, n = u // 2, u % 2, n_keys(u)
                    pe.wait_ge(unit_PT, 16 * i + u + 1)
                    if u == 0:
                        pe.wait_ge(av_loaded, 16 * i + 16)
                    dst = ps[:, (6 + hd) * HALF + t * DH:(6 + hd) * HALF + (t + 1) * DH]
                    for c in range(n):
                        mm = pe.matmul(dst, PT[:, u % 2, c * P:(c + 1) * P],
                                       vin[:, t - n + 1 + c, hd * DH:(hd + 1) * DH],
                                       start=(c == 0), stop=(c == n - 1))
                    mm.then_inc(unit_out, 1)

                for u in range(16 + 2):
                    if u < 16:
                        scores(u)
                    if 1 <= u <= 16:
                        turn(u - 1)
                    if u >= 2:
                        values(u - 2)

            pe.wait_ge(proj_evac, 56)
            pe.wait_ge(ro_ready, HH + 1)
            with pe.Fori(0, AH // 2) as i:
                pair(i)

            turn_tile(R_CAT, 0)
            turn_tile(R_CAT, 1)
            for h in range(2):
                for t in range(TT):
                    d = A_OUT + 8 * h + t
                    if h == 0:
                        pe.wait_ge(hT_ready, TT * R_CAT + t + 1)
                    if 8 * h + t >= 4:
                        pe.wait_ge(x_added, d - 3)
                    for k in range(KT):
                        s = (P_OUT + 4 * h + k // 2) % RING
                        if t == 0 and k % 2 == 0:
                            pe.wait_ge(split_lo, P_OUT + 4 * h + k // 2 + 1)
                        c0 = (k % 2) * HALF
                        mm = three(bank(4 + d % 4), [a[:, k, t * P:(t + 1) * P] for a in (hThi, hTlo)],
                                   [w[:, s, c0:c0 + HALF] for w in (whi, wlo)], k == 0, k == KT - 1)
                        if t == TT - 1 and k % 2 == 1 and k < KT - 1:
                            mm.then_inc(piece_used, 1)
                    mm.then_inc(row_done, 1)
                    if h == 0 and t + 2 < TT:
                        turn_tile(R_CAT, t + 2)
                    if h == 1 and t >= 2:
                        turn_tile(R_FFN2, t - 2)
            turn_tile(R_FFN2, TT - 2)
            turn_tile(R_FFN2, TT - 1)
            ffn(1, P_FFN2, A_FFN2, R_FFN2)

        @block.scalar
        def _(act):
            def split(n0, adv=0):
                s = n0 % RING
                act.wait_ge(raw_loaded[s], 16 * (n0 // RING + 1) + 4 * adv)
                act.activation(whi[:, s, :], raw[:, s, :], ACT.Copy).then_inc(split_hi, 1)

            def square(R, t):
                q = TT * norm_no(R) + t
                if R == R_FFN1:
                    act.wait_ge(x_loaded[t], 16)
                elif R == R_MIX:
                    act.wait_ge(x_added, A_FFN1 + ADDS_FFN - 16 + 2 * t + 2)
                else:
                    act.wait_ge(x_added, A_OUT + 8 + t + 1)
                if q:
                    act.wait_ge(ss_ready, q)
                if R == R_FFN2 and t == 0:
                    act.wait_ge(qk_ss, AH + 1)
                act.activation(junk[:, :], xs[:, t, :], ACT.Square,
                               accum_out=ss[:, q:q + 1]).then_inc(ss_ready, 1)

            def hT_hi(R, t):
                r = TT * R + t
                act.wait_ge(turned, r + 1)
                src = ps[:, (t % 2) * 1024:(t % 2 + 1) * 1024].rearrange("p (k c) -> p k c", k=KT)
                act.activation(hThi[:, :, t * P:(t + 1) * P], src, ACT.Copy).then_inc(hT_hi_ready, 1)

            def used(group, q, advn=0):
                if q < 3:
                    act.wait_ge(piece_used, 3 * group + q + 1 + 3 * advn)
                elif group < 7:
                    act.wait_ge(proj_done, 8 * group + 8 + 8 * advn)
                else:
                    act.wait_ge(row_done, A_OUT + 8 * (group - 7) + 8)

            def ffn(F, base, adds, tail):
                e_base = 2 * FT * F

                def tile(f0, advf, n0, adv):
                    for h in range(2):
                        e = e_base + 2 * f0 + h
                        act.wait_ge(gate_done, e + 1 + 2 * advf)
                        if e >= 2:
                            act.wait_ge(prod_done, e - 1 + 2 * advf)
                        act.activation(sil[:, h, :], bank(h), ACT.Silu).then_inc(silu_done, 1)
                        if h == 0:
                            split(n0 + 2, adv)
                    split(n0 + 3, adv)
                    for h in range(2):
                        e = e_base + 2 * f0 + h
                        act.wait_ge(prod_done, e + 1 + 2 * advf)
                        act.activation(hidhi[:, (f0 // 2) % 2, f0 % 2, h * HALF:(h + 1) * HALF],
                                       prod[:, h, :], ACT.Copy).then_inc(hid_hi_ready, 1)

                tile(0, 0, base, 0)
                tile(1, 0, base + 2, 0)
                with act.Fori(0, NG // 2) as i:
                    for g in range(2):
                        n0 = base + 4 + 6 * g
                        tile(2 + 2 * g, 4 * i, n0, 12 * i)
                        tile(3 + 2 * g, 4 * i, n0 + 2, 12 * i)
                        last = g == 1
                        split(n0 + 6, 12 * i)
                        split(n0 + 7, 12 * i)
                if tail:
                    act.wait_ge(row_done, adds + 16 * (NG - 1))
                    split(base + PIECES_FFN)
                    split(base + PIECES_FFN + 1)
                    for t in range(TT + 2):
                        if t < TT:
                            square(R_MIX, t)
                        if t >= 2:
                            hT_hi(R_MIX, t - 2)

            for t in range(1, TT):
                act.dma_start(xs[:, t, :], x[0, t * P:(t + 1) * P, :]).then_inc(x_loaded[t], 16)
            for t in range(TT + 2):
                if t < TT:
                    square(R_FFN1, t)
                if t >= 2:
                    hT_hi(R_FFN1, t - 2)
                if t == 3:
                    split(0)
                if t == 5:
                    split(1)
            ffn(0, P_FFN1, A_FFN1, True)

            def stage(o):
                return y[:, (o // 2) % 2, (o % 2) * HALF:(o % 2 + 1) * HALF]

            def evac(n0, advn, o, func):
                idx = 8 * n0 + o
                act.wait_ge(proj_done, idx + 1 + 8 * advn)
                if idx >= 4:
                    act.wait_ge(proj_stored[o % 4], 16 * (idx // 4) + 32 * advn)
                if func == ACT.Sigmoid:
                    act.activation(stage(o), bank(4 + o % 4), ACT.Sigmoid).then_inc(sig_ready, 1)
                    act.wait_ge(sig_ready, o + 1)
                    act.activation(stage(o), stage(o), ACT.Identity, scale=lb[:, 1, o // 2:o // 2 + 1],
                                   bias=lb[:, 0, o // 2:o // 2 + 1]).then_inc(proj_evac, 1)
                else:
                    act.activation(stage(o), bank(4 + o % 4), func).then_inc(proj_evac, 1)

            def store(n0, advn, o, feature):
                idx = 8 * n0 + o
                act.wait_ge(proj_evac, idx + 1 + 8 * advn)
                if feature:
                    row = n0 * HALF + (o // 2) * P
                    dst = feat[row:row + P, (o % 2) * HALF:(o % 2 + 1) * HALF]
                else:
                    dst = tok[o * P:(o + 1) * P, ds(n0 - 2 + advn, 1), :].rearrange("p a c -> p (a c)")
                act.dma_start(dst, stage(o)).then_inc(proj_stored[o % 4], 16)

            def group(n0, advn, func, feature=False, head=None):
                for o in range(7):
                    evac(n0, advn, o, func)
                    store(n0, advn, o, feature)
                if head is not None:
                    act.wait_ge(k_turned, head + 2)
                    act.activation(kS[:, :, :].rearrange("p a b -> p (a b)"), ps[:, 0:1024], ACT.Copy)\
                       .then_inc(k_rows, 1)
                for q in range(4):
                    used(n0, q, advn)
                    split(P_MIX + 4 * n0 + 4 + q, 4 * advn)
                evac(n0, advn, 7, func)
                store(n0, advn, 7, feature)
                if head is not None:
                    act.wait_ge(read_done, head + 2)
                    act.wait_ge(read_ss, head + 1)
                    act.wait_ge(ss_ready, 2 * TT)
                    act.activation(junk[:, :], ps[:, 0:1024], ACT.Square).then_inc(read_sq, 1)

            act.wait_ge(row_done, A_OUT)
            split(P_MIX + 2)
            split(P_MIX + 3)
            group(0, 0, ACT.Silu, True)
            act.wait_ge(lb_diff, 1)
            act.activation(lb[:, 0, :], lb[:, 2, :], ACT.Sigmoid).then_inc(lb_sig, 1)
            act.wait_ge(lb_ready, 1)
            group(1, 0, ACT.Sigmoid, True)
            group(2, 0, ACT.Copy)
            group(3, 0, ACT.Silu, head=0)
            with act.Fori(1, HH) as j:
                group(3, j, ACT.Copy, head=j)

            def pair(i):
                for w, src in ((0, qin), (1, kin)):
                    act.wait_ge(qk_loaded, 32 * i + 32)
                    act.wait_ge(qk_ss, 2 * i + w + 1)
                    act.activation(junk[:, :], src[:, :, :].rearrange("p a b -> p (a b)"),
                                   ACT.Square).then_inc(qk_sq, 1)
                for w, dst in ((0, qT), (1, kT)):
                    act.wait_ge(qk_turned, 2 * i + w + 1)
                    act.activation(dst[:, :], ps[:, 2 * w * HALF:2 * w * HALF + T], ACT.Copy,
                                   scale=qkg[:, w:w + 1]).then_inc(qkT_ready, 1)

                for u in range(16):
                    n = min(u // 2 + 1, KEY_TILES) * P
                    act.wait_ge(unit_max, 16 * i + u + 1)
                    if u >= 2:
                        act.wait_ge(unit_turned, 16 * i + u - 1)
                    act.activation(Pr[:, u % 2, 0:n], S[:, u % 2, 0:n], ACT.Exp, scale=-1.0,
                                   bias=nmax[:, u % 2, u // 2:u // 2 + 1],
                                   accum_out=psumr[:, u % 2, u // 2:u // 2 + 1]).then_inc(unit_exp, 1)

            with act.Fori(0, AH // 2) as i:
                pair(i)

            for t in range(TT):
                hT_hi(R_CAT, t)
            for q in range(4):
                used(7, q)
                split(P_OUT + 4 + q)
            for t in range(TT + 2):
                if t < TT:
                    square(R_FFN2, t)
                if t == TT - 1:
                    for q in range(2):
                        used(8, q)
                        split(P_FFN2 + q)
                if t >= 2:
                    hT_hi(R_FFN2, t - 2)
            ffn(1, P_FFN2, A_FFN2, False)
            for t in range(TT):
                act.wait_ge(x_added, A_FFN2 + ADDS_FFN - 16 + 2 * t + 2)
                act.dma_start(out[0, t * P:(t + 1) * P, :], xs[:, t, :]).then_inc(out_stored, 16)
            act.wait_ge(out_stored, 16 * TT)

        @block.vector
        def _(dve):
            def split(n0, adv=0):
                s = n0 % RING
                dve.wait_ge(split_hi, n0 + 1 + adv)
                dve.tensor_tensor(wlo[:, s, :], raw[:, s, :], whi[:, s, :].bitcast(F32), ALU.subtract)\
                   .then_inc(split_lo, 1)

            def normalise(R, t):
                q = TT * norm_no(R) + t
                dve.wait_ge(rstd_ready, q + 1)
                if t == 0:
                    dve.wait_ge(gain_loaded, 16 * norm_no(R) + 16)
                if t >= 2:
                    dve.wait_ge(turned, TT * R + t - 1)
                dve.scalar_tensor_tensor(y[:, t % 2, :], xs[:, t, :], rstd[:, q:q + 1], gain[:, :],
                                         ALU.mult, ALU.mult).then_inc(y_ready, 1)

            def hT_lo(R, t):
                r = TT * R + t
                dve.wait_ge(hT_hi_ready, r + 1)
                src = ps[:, (t % 2) * 1024:(t % 2 + 1) * 1024].rearrange("p (k c) -> p k c", k=KT)
                dve.tensor_tensor(hTlo[:, :, t * P:(t + 1) * P], src,
                                  hThi[:, :, t * P:(t + 1) * P].bitcast(F32), ALU.subtract)\
                   .then_inc(hT_ready, 1)

            def add(d0, advd, t, h, scale):
                dve.wait_ge(row_done, d0 + 1 + advd)
                dst = xs[:, t, h * HALF:(h + 1) * HALF]
                dve.scalar_tensor_tensor(dst, bank(4 + d0 % 4), scale, dst, ALU.mult, ALU.add)\
                   .then_inc(x_added, 1)

            def ffn(F, base, adds, tail):
                e_base = 2 * FT * F

                def tile(f0, advf, n0, adv):
                    split(n0 + 2, adv)
                    split(n0 + 3, adv)
                    for h in range(2):
                        e = e_base + 2 * f0 + h
                        dve.wait_ge(silu_done, e + 1 + 2 * advf)
                        dve.wait_ge(up_done, e + 1 + 2 * advf)
                        if e >= 2:
                            dve.wait_ge(hid_ready, e - 1 + 2 * advf)
                        dve.tensor_tensor(prod[:, h, :], bank(2 + h), sil[:, h, :], ALU.mult)\
                           .then_inc(prod_done, 1)
                    for h in range(2):
                        e = e_base + 2 * f0 + h
                        dve.wait_ge(hid_hi_ready, e + 1 + 2 * advf)
                        at = (slice(None), (f0 // 2) % 2, f0 % 2, slice(h * HALF, (h + 1) * HALF))
                        dve.tensor_tensor(hidlo[at], prod[:, h, :], hidhi[at].bitcast(F32), ALU.subtract)\
                           .then_inc(hid_ready, 1)

                tile(0, 0, base, 0)
                tile(1, 0, base + 2, 0)
                with dve.Fori(0, NG // 2) as i:
                    for g in range(2):
                        n0 = base + 4 + 6 * g
                        tile(2 + 2 * g, 4 * i, n0, 12 * i)
                        tile(3 + 2 * g, 4 * i, n0 + 2, 12 * i)
                        for t in range(TT):
                            for h in range(2):
                                add(adds + 16 * g + 2 * t + h, 32 * i, t, h, 0.5)
                            if t in (1, 3):
                                split(n0 + 6 + t // 2, 12 * i)
                d0 = adds + 16 * (NG - 1)
                if tail:
                    split(base + PIECES_FFN)
                    split(base + PIECES_FFN + 1)
                for t in range(TT):
                    for h in range(2):
                        add(d0 + 2 * t + h, 0, t, h, 0.5)
                    if tail:
                        if t >= 1:
                            normalise(R_MIX, t - 1)
                        if t >= 2:
                            hT_lo(R_MIX, t - 2)
                if tail:
                    normalise(R_MIX, TT - 1)
                    hT_lo(R_MIX, TT - 2)
                    hT_lo(R_MIX, TT - 1)

            for t in range(TT + 2):
                if t < TT:
                    normalise(R_FFN1, t)
                if t >= 2:
                    hT_lo(R_FFN1, t - 2)
                if t == 5:
                    split(0)
                if t == 7:
                    split(1)
            ffn(0, P_FFN1, A_FFN1, True)

            split(P_MIX + 2)
            split(P_MIX + 3)
            dve.wait_ge(lb_loaded, 16)
            dve.tensor_tensor(lb[:, 2, :], lbs[:, 0, :], lbs[:, 1, :], ALU.subtract).then_inc(lb_diff, 1)
            for q in range(4):
                split(P_MIX + 4 + q)
            dve.wait_ge(lb_sig, 1)
            dve.tensor_scalar(lb[:, 1, :], lb[:, 0, :], -1.0, 1.0, ALU.mult, ALU.add).then_inc(lb_ready, 1)
            for n in (1, 2):
                for q in range(4):
                    split(P_MIX + 4 * n + 4 + q)

            def head(j):
                n = [0]

                def link(ins):
                    n[0] += 1
                    ins.then_inc(hgrn_step, 1)
                    dve.wait_ge(hgrn_step, n[0] + per_head * j)

                def keep_scores(L):
                    if L:
                        dve.wait_ge(mask_set, LEVELS - 1)
                    dve.wait_ge(scores_done, 8 * j + L + 1)
                    if L == 0:
                        dst = aT[:, :].rearrange("p (c t) -> p c t", c=TT)
                        src = ps[:, 0:1024].rearrange("p (c t) -> p c t", c=TT)
                        eye = bass.AP(ident, 0, [list(ident[:, :].ap[0]), [0, TT], [1, P]])
                        dve.tensor_tensor(dst, src, eye, ALU.mult).then_inc(scores_kept, 1)
                        return
                    dve.wait_ge(scores_kept, 8 * j + L)
                    h = 1 << (L - 1)
                    dst = aT[:, :].rearrange("p (b two h) -> p b two h", two=2, h=h)[:, :, 1, :]
                    src = bank(2 + L % 2).rearrange("p (b h) -> p b h", h=h)
                    m = mk[:, (L - 1) * HALF:L * HALF].rearrange("p (b h) -> p b h", h=h)
                    dve.copy_predicated(dst, m, src).then_inc(scores_kept, 1)

                dve.wait_ge(fq_loaded, 32 * j + 32)
                dve.wait_ge(k_turned, j + 1)
                dve.tensor_scalar(hK[:, :], fF[:, :], -1.0, 1.0, ALU.mult, ALU.add).then_inc(scaled, 1)
                dve.wait_ge(read_done, j + 1)
                link(dve.tensor_tensor(hQ[:, :], fQ[:, :], fF[:, :], ALU.mult))
                dve.wait_ge(scaled, 9 * j + 1)
                dve.nop().then_inc(scaled, 1)
                keep_scores(0)
                before, size = fF[:, :], T
                used = 0
                for L in range(2, LEVELS + 1):
                    s = 1 << (L - 2)
                    tt = before.rearrange("p (b two) -> p b two", two=2)
                    kk = hK[:, :].rearrange("p (b two s) -> p b two s", two=2, s=s)
                    qq = hQ[:, :].rearrange("p (b two s) -> p b two s", two=2, s=s)
                    nb = T // (2 * s)
                    after = tot[:, used:used + nb]
                    used += nb
                    dve.wait_ge(scores_done, 8 * j + L)
                    link(dve.tensor_tensor(kk[:, :, 0, :], kk[:, :, 0, :],
                                           tt[:, :, 1:2].to_broadcast([P, nb, s]), ALU.mult))
                    link(dve.tensor_tensor(qq[:, :, 1, :], qq[:, :, 1, :],
                                           tt[:, :, 0:1].to_broadcast([P, nb, s]), ALU.mult))
                    link(dve.tensor_tensor(after, tt[:, :, 0], tt[:, :, 1], ALU.mult))
                    dve.nop().then_inc(scaled, 1)
                    keep_scores(L - 1)
                    before = after
                dve.wait_ge(outer_done, j + 1)
                for c in range(TT - 1):
                    kv = ps[:, 2 * HALF + c * P:2 * HALF + (c + 1) * P]
                    if c == 0:
                        dve.tensor_copy(st[:, 1, :], kv).then_inc(state_step, 1)
                    else:
                        dve.wait_ge(state_step, 7 * j + c)
                        dve.scalar_tensor_tensor(st[:, c + 1, :], st[:, c, :], before[:, c:c + 1], kv,
                                                 ALU.mult, ALU.add).then_inc(state_step, 1)
                for q in range(4):
                    split(P_MIX + 16 + q, 4 * j)
                dve.wait_ge(read_sq, j + 1)
                dve.tensor_reduce(sso[:, :], junk[:, :].rearrange("p (c v) -> p c v", c=TT), AX_X,
                                  ALU.add).then_inc(read_ss, 1)
                dve.wait_ge(read_rstd, j + 1)
                dve.wait_ge(gate_gained, j + 1)
                for c in range(TT):
                    last = dve.scalar_tensor_tensor(hG[:, c, :], ps[:, c * P:(c + 1) * P], rso[:, c:c + 1],
                                                    hG[:, c, :], ALU.mult, ALU.mult)
                last.then_inc(ro_ready, 1)

            per_head = 1 + 3 * 7
            dve.wait_ge(mask_loaded, 16)
            for L in range(LEVELS - 1):
                m = bass.AP(tot, L * 64, [list(tot[:, :].ap[0]), [0, TT], [1, 64]])
                dve.tensor_copy(mk[:, L * HALF:(L + 1) * HALF].rearrange("p (c t) -> p c t", c=TT), m)\
                   .then_inc(mask_set, 1)
            dve.nop().then_inc(read_ss, 1)
            dve.nop().then_inc(ro_ready, 1)
            with dve.Fori(0, HH) as j:
                head(j)

            dve.wait_ge(rel_loaded, 16)
            n_far = EXT - 1 - (REL_CLIP + 127)
            dve.tensor_copy(extrow[:, n_far:EXT - 1], relrow[:, N_REL - 2:0:-1]).then_inc(ext_step, 1)
            dve.tensor_copy(extrow[:, 0:n_far], relrow[:, N_REL - 1:N_REL].to_broadcast([AH, n_far]))\
               .then_inc(ext_step, 1)
            dve.memset(extrow[:, EXT - 1:EXT], 0.0).then_inc(ext_step, 1)
            dve.wait_ge(qk_gain_loaded, 64)
            dve.tensor_scalar(qkg[:, 0:1], qkg[:, 0:1], DH ** -0.5, None, ALU.mult).then_inc(qk_gain_ready, 1)
            dve.nop().then_inc(qk_ss, 1)

            def pair(i):
                for w, src in ((0, qin), (1, kin)):
                    dve.wait_ge(qk_sq, 2 * i + w + 1)
                    dve.tensor_reduce(ssq[:, w, :], junk[:, :].rearrange("p (g d) -> p g d", d=DH), AX_X,
                                      ALU.add).then_inc(qk_ss, 1)
                for w, src in ((0, qin), (1, kin)):
                    dve.wait_ge(qk_rstd, 2 * i + w + 1)
                    v = src[:, :, :].rearrange("p t (h d) -> p (t h) d", d=DH)
                    r = rsq[:, w, :].unsqueeze(2).to_broadcast([P, 16, DH])
                    dve.tensor_tensor(v, v, r, ALU.mult).then_inc(qk_normed, 1)

                def unit_head(u):
                    n = min(u // 2 + 1, KEY_TILES) * P
                    dve.wait_ge(unit_scores, 16 * i + u + 1)
                    if u == 0:
                        dve.wait_ge(bias_masked, 4 * i + 4)
                    if u >= 2:
                        dve.wait_ge(unit_exp, 16 * i + u - 1)
                    dve.nop().then_inc(dve_passed, 1)
                    dve.tensor_tensor_reduce(S[:, u % 2, 0:n], ps[:, 2 * (u % 2) * HALF:2 * (u % 2) * HALF + n],
                                             bias[:, u % 2, BAND - n:BAND], -1.0, 3.0e38, ALU.add, ALU.min,
                                             nmax[:, u % 2, u // 2:u // 2 + 1]).then_inc(unit_max, 1)

                def unit_tail(u):
                    n = min(u // 2 + 1, KEY_TILES) * P
                    dve.wait_ge(unit_turned, 16 * i + u + 1)
                    if u >= 2:
                        dve.wait_ge(unit_out, 16 * i + u - 1)
                    dve.tensor_copy(PT[:, u % 2, 0:n], ps[:, 4 * HALF:4 * HALF + n]).then_inc(unit_PT, 1)

                for u in range(17):
                    if u < 16:
                        unit_head(u)
                    if u >= 1:
                        unit_tail(u - 1)
                for hd in range(2):
                    dve.wait_ge(unit_exp, 16 * i + 16)
                    dve.reciprocal(rcp[:, hd, :], psumr[:, hd, :]).then_inc(rcp_ready, 1)
                    dve.wait_ge(unit_out, 16 * i + 15 + hd)
                    dve.wait_ge(rcp_ready, 2 * i + hd + 1)
                    dve.tensor_tensor(cat[:, :, ds((2 * i + hd) * DH, DH)],
                                      bank(6 + hd).rearrange("p (t d) -> p t d", d=DH),
                                      rcp[:, hd, :].unsqueeze(2).to_broadcast([P, TT, DH]), ALU.mult)\
                       .then_inc(head_out, 1)

            dve.wait_ge(ro_stored, 16 * HH)
            with dve.Fori(0, AH // 2) as i:
                pair(i)

            hT_lo(R_CAT, 0)
            hT_lo(R_CAT, 1)
            for t in range(TT):
                if t == TT - 1:
                    for q in range(4):
                        split(P_OUT + 4 + q)
                add(A_OUT + t, 0, t, 0, 1.0)
                if t + 2 < TT:
                    hT_lo(R_CAT, t + 2)
            for t in range(TT):
                add(A_OUT + 8 + t, 0, t, 1, 1.0)
                if t >= 1:
                    normalise(R_FFN2, t - 1)
                if t == TT - 1:
                    split(P_FFN2)
                    split(P_FFN2 + 1)
                if t >= 2:
                    hT_lo(R_FFN2, t - 2)
            normalise(R_FFN2, TT - 1)
            hT_lo(R_FFN2, TT - 2)
            hT_lo(R_FFN2, TT - 1)
            ffn(1, P_FFN2, A_FFN2, False)

        @block.gpsimd
        def _(pool):
            pool.memset(mhalf[:, :], -0.5).then_inc(mhalf_set, 1)
            pool.dma_start(ident[:, :], identity).then_inc(ident_loaded, 16)
            pool.dma_start(gain[:, :], ffn1_norm_g[0:1, :].to_broadcast([P, D])).then_inc(gain_loaded, 16)
            pool.dma_start(lbs[:, :, :], hgrn_lower_bounds.rearrange("r (h p) -> p r h", p=P),
                           allow_slow_non_contiguous=True).then_inc(lb_loaded, 16)
            pool.dma_start(gn[:, :], hgrn_out_norm_g[0:1, :].to_broadcast([P, P])).then_inc(gn_loaded, 16)
            pool.dma_start(qkg[0:DH, 0:1], attn_q_norm_g.rearrange("a d -> d a"),
                           allow_slow_non_contiguous=True).then_inc(qk_gain_loaded, 16)
            pool.dma_start(qkg[DH:P, 0:1], attn_q_norm_g.rearrange("a d -> d a"),
                           allow_slow_non_contiguous=True).then_inc(qk_gain_loaded, 16)
            pool.dma_start(qkg[0:DH, 1:2], attn_k_norm_g.rearrange("a d -> d a"),
                           allow_slow_non_contiguous=True).then_inc(qk_gain_loaded, 16)
            pool.dma_start(qkg[DH:P, 1:2], attn_k_norm_g.rearrange("a d -> d a"),
                           allow_slow_non_contiguous=True).then_inc(qk_gain_loaded, 16)
            pool.wait_ge(mhalf_set, 1)

            def rms(R):
                for t in range(TT):
                    q = TT * norm_no(R) + t
                    pool.wait_ge(ss_ready, q + 1)
                    pool.tensor_scalar(rstd[:, q:q + 1], ss[:, q:q + 1], 1.0 / D, EPS, ALU.mult, ALU.add)\
                        .then_inc(var_ready, 1)
                    pool.wait_ge(var_ready, q + 1)
                    pool.tensor_tensor(rstd[:, q:q + 1], rstd[:, q:q + 1], mhalf[:, 0:1], ALU.pow)\
                        .then_inc(rstd_ready, 1)

            rms(R_FFN1)
            pool.wait_ge(y_ready, TT)
            pool.dma_start(gain[:, :], mix_norm_g[0:1, :].to_broadcast([P, D])).then_inc(gain_loaded, 16)
            rms(R_MIX)
            pool.wait_ge(y_ready, 2 * TT)
            pool.dma_start(gain[:, :], ffn2_norm_g[0:1, :].to_broadcast([P, D])).then_inc(gain_loaded, 16)

            def stored(n):
                for s in range(4):
                    pool.wait_ge(proj_stored[s], 32 * n)

            def load_fq(j):
                pool.dma_start(fF[:, :], feat[ds(j * P + HALF, P), :]).then_inc(fq_loaded, 16)
                pool.dma_start(fQ[:, :], feat[ds(j * P, P), :]).then_inc(fq_loaded, 16)

            def load_v(j):
                pool.dma_start(hV[:, :, :], tok[:, 0, ds(j * P, P)].rearrange("(t p) c -> p t c", p=P))\
                    .then_inc(v_loaded, 16)

            def load_g(j):
                pool.dma_start(hG[:, :, :], tok[:, 1, ds(j * P, P)].rearrange("(t p) c -> p t c", p=P))\
                    .then_inc(g_loaded, 16)

            def finish(j):
                pool.wait_ge(gn_loaded, 16)
                pool.wait_ge(g_loaded, 16 * j + 16)
                gb = bass.AP(gn, 0, [list(gn[:, :].ap[0]), [0, TT], [1, P]])
                pool.tensor_tensor(hG[:, :, :], hG[:, :, :], gb, ALU.mult).then_inc(gate_gained, 1)
                pool.wait_ge(read_ss, j + 2)
                pool.nop().then_inc(pool_passed, 1)
                pool.tensor_scalar(rso[:, :], sso[:, :], 1.0 / P, EPS, ALU.mult, ALU.add).then_inc(read_var, 1)
                pool.wait_ge(read_var, j + 1)
                pool.tensor_tensor(rso[:, :], rso[:, :], mhalf[:, 0:TT], ALU.pow).then_inc(read_rstd, 1)
                pool.wait_ge(ro_ready, j + 2)
                pool.dma_start(ro_d[:, ds(j * P, P)].rearrange("(t p) c -> p t c", p=P), hG[:, :, :])\
                    .then_inc(ro_stored, 16)

            pool.wait_ge(x_added, A_OUT)
            pool.dma_start(tot[:, 0:(LEVELS - 1) * 64], masks).then_inc(mask_loaded, 16)
            stored(2)
            load_fq(0)
            stored(3)
            load_v(0)
            stored(4)
            load_g(0)
            with pool.Fori(0, HH - 1) as j:
                pool.wait_ge(scores_done, 8 * j + 1)
                pool.wait_ge(scaled, 9 * j + 3)
                load_fq(j + 1)
                finish(j)
                pool.wait_ge(read_done, j + 2)
                load_v(j + 1)
                pool.wait_ge(ro_stored, 16 * j + 16)
                load_g(j + 1)
            finish(HH - 1)

            pool.wait_ge(proj_done, 56)
            pool.dma_start(relrow[:, :], attn_rel_bias[0]).then_inc(rel_loaded, 16)
            pool.wait_ge(ext_step, 3)
            pool.dma_start(ext_d, extrow[:, :]).then_inc(ext_stored, 16)
            pool.wait_ge(ext_stored, 16)
            skew = bass.AP(ext_d.tensor, P - 1, [[EXT, AH], [-1, P], [1, BAND]])
            pool.dma_start(bias_d, skew).then_inc(bias_stored, 16)
            pool.wait_ge(bias_stored, 16)
            stored(7)
            pool.wait_ge(ro_stored, 16 * HH)
            pool.dma_start(cat[:, :, HALF:D], ro_d.rearrange("(t p) c -> p t c", p=P)).then_inc(cat_loaded, 16)

            def load_pair(i):
                for g, dst in ((2, qin), (3, kin)):
                    pool.dma_start(dst[:, :, :], tok[:, g, ds(i * P, P)].rearrange("(t p) c -> p t c", p=P))\
                        .then_inc(qk_loaded, 16)
                pool.dma_start(vin[:, :, :], tok[:, 4, ds(i * P, P)].rearrange("(t p) c -> p t c", p=P))\
                    .then_inc(av_loaded, 16)
                pool.dma_start(bias[:, :, :], bias_d[ds(2 * i, 2), :, :].rearrange("h t s -> t h s"))\
                    .then_inc(bias_loaded, 16)
                pool.wait_ge(bias_loaded, 16 * i + 16)
                pool.nop().then_inc(pool_passed, 1)
                for hd in range(2):
                    pool.memset(bias[CHUNK:P, hd, 0:CHUNK], MASKED).then_inc(bias_masked, 1)
                    pool.memset(bias[0:CHUNK, hd, BAND - CHUNK:BAND], MASKED).then_inc(bias_masked, 1)

            def qk_rms(i):
                for w in range(2):
                    pool.wait_ge(bias_masked, 4 * i + 4)
                    pool.wait_ge(qk_ss, 2 * i + w + 2)
                    pool.nop().then_inc(pool_passed, 1)
                    pool.tensor_scalar(rsq[:, w, :], ssq[:, w, :], 1.0 / DH, EPS, ALU.mult, ALU.add)\
                        .then_inc(qk_var, 1)
                    pool.wait_ge(qk_var, 2 * i + w + 1)
                    pool.tensor_tensor(rsq[:, w, :], rsq[:, w, :], mhalf[:, 0:16], ALU.pow).then_inc(qk_rstd, 1)

            load_pair(0)
            with pool.Fori(0, AH // 2 - 1) as i:
                qk_rms(i)
                pool.wait_ge(unit_out, 16 * i + 16)
                load_pair(i + 1)
            qk_rms(AH // 2 - 1)
            rms(R_FFN2)


_NAMES = ["x", "ffn1_norm_g", "ffn1_w_gate", "ffn1_w_up", "ffn1_w_down", "mix_norm_g", "w_in",
          "attn_q_norm_g", "attn_k_norm_g", "attn_rel_bias", "hgrn_lower_bounds", "hgrn_out_norm_g",
          "w_out", "ffn2_norm_g", "ffn2_w_gate", "ffn2_w_up", "ffn2_w_down"]


def kernel(**inputs):
    import concourse.bacc as bacc
    from concourse.bass_utils import run_bass_kernel_spmd

    nc = bacc.Bacc("TRN2", target_bir_lowering=False, num_devices=1)
    arrays = {n: np.ascontiguousarray(inputs[n]) for n in _NAMES}
    arrays["identity"] = np.eye(P, dtype=np.float32)
    arrays["masks"] = level_masks()
    args = [nc.dram_tensor(n, a.shape, mybir.dt.from_np(a.dtype), kind="ExternalInput").ap()
            for n, a in arrays.items()]
    out = nc.dram_tensor("out", (1, T, D), F32, kind="ExternalOutput").ap()
    build(nc, *args, out)
    r = run_bass_kernel_spmd(nc, [arrays], core_ids=[0])
    return r.results[0]["out"]
```

```python
from contextlib import ExitStack

import numpy as np

import concourse.bass as bass
from concourse import mybir

F32 = mybir.dt.float32
F32R = mybir.dt.float32r
U8 = mybir.dt.uint8
ALU = mybir.AluOpType
ACT = mybir.ActivationFunctionType
AX_X = mybir.AxisListType.X

P = 128
T = 1024
D = 1024
TT = T // P
KT = D // P
HALF = 512
D_FF = 2816
FT = D_FF // P
NG = FT // 2
AH = 8
DH = 64
AW = AH * DH
HH = 4
CHUNK = 64
KEY_TILES = 5
BAND = KEY_TILES * P
N_REL = 257
REL_CLIP = 128
EXT = 768
EPS = 1e-6
MASKED = -1.0e30

RING = 4
PIECES_FFN = 3 * FT
PIECES_MIX = 4 * 7
PIECES_OUT = 8
P_FFN1 = 0
P_MIX = P_FFN1 + PIECES_FFN
P_OUT = P_MIX + PIECES_MIX
P_FFN2 = P_OUT + PIECES_OUT

ADDS_FFN = NG * 16
A_FFN1 = 0
A_OUT = A_FFN1 + ADDS_FFN
A_FFN2 = A_OUT + 16

R_FFN1, R_MIX, R_CAT, R_FFN2 = range(4)

LEVEL_AT = {2: 0, 3: 1, 5: 2, 6: 3, 8: 4, 9: 5, 10: 6, 12: 7}
TURN_AT, OUTER_AT, READ_AT = 13, 14, 15
LEVELS = 8

FEATURE_ORDER = [(0, 0), (1, 0), (0, 1), (1, 1), (2, 0), (3, 0), (2, 1), (3, 1)]

UNITS = [[(7, 5, 0)], [(6, 5, 0)], [(5, 5, 0)], [(4, 5, 0)],
         [(3, 4, 0), (0, 1, 4 * P)], [(2, 3, 0), (1, 2, 3 * P)]]
NU = 2 * len(UNITS)
SQUARE_AT, SUM_AT, NORM_AT, TURN_QK_AT = (2, 3), (4, 5), (6, 7), (8, 10)


def unit(v):
    return v // NU, v % 2, UNITS[(v % NU) // 2]


def by_scalar(v):
    return v % 3 == 2


def turn_bank(R, t):
    if R == R_FFN1:
        return 2 * (t % 2) + (4 if t >= 4 else 0)
    if R == R_FFN2:
        return 4 if t == 7 else 2 * ((t + 1) % 2)
    return 2 * (t % 2)


def level_masks():
    m = np.zeros((P, LEVELS - 1, P // 2), np.float32)
    for level in range(1, LEVELS):
        h = 1 << (level - 1)
        for b in range(P // (2 * h)):
            m[2 * h * b:2 * h * b + h, level - 1, b * h:(b + 1) * h] = 1
    return m.reshape(P, -1)


def build(nc, x, ffn1_norm_g, ffn1_w_gate, ffn1_w_up, ffn1_w_down, mix_norm_g, w_in, attn_q_norm_g,
          attn_k_norm_g, attn_rel_bias, hgrn_lower_bounds, hgrn_out_norm_g, w_out, ffn2_norm_g,
          ffn2_w_gate, ffn2_w_up, ffn2_w_down, identity, masks, out):
    ds = bass.DynSlice
    with ExitStack() as ctx:
        feat = nc.dram_tensor("feat_scratch", [2 * HH * P, T], F32, kind="Internal").ap()
        tok = nc.dram_tensor("tok_scratch", [T, 5, HALF], F32, kind="Internal").ap()
        ro_d = nc.dram_tensor("ro_scratch", [T, HALF], F32, kind="Internal").ap()
        bias_d = nc.dram_tensor("bias_scratch", [AH, P, BAND], F32, kind="Internal").ap()
        ext_d = nc.dram_tensor("ext_scratch", [AH, EXT], F32, kind="Internal").ap()

        def keep(name, shape, dt=F32, where=ctx, side="left"):
            return where.enter_context(nc.sbuf_tensor(name, shape, dt, side=side))

        def sem(name):
            return ctx.enter_context(nc.semaphore(name))

        xs = keep("xs", [P, TT, D])
        raw = keep("raw", [P, RING, 1024])
        whi = keep("whi", [P, RING, 1024], F32R)
        wlo = keep("wlo", [P, RING, 1024], F32R)
        y = keep("y", [P, 2, D])
        junk = keep("junk", [P, 1024])
        gain = keep("gain", [P, D])
        ident = keep("ident", [P, P])
        ss = keep("ss", [P, 3 * TT])
        rstd = keep("rstd", [P, 3 * TT])
        mhalf = keep("mhalf", [P, 16])
        lbs = keep("lbs", [P, 2, HH])
        lb = keep("lb", [P, 3, HH])
        gn = keep("gn", [P, P])
        qkg = keep("qkg", [P, 2])
        ssq = keep("ssq", [P, 2, 16])
        rsq = keep("rsq", [P, 2, 16])

        with ExitStack() as c:
            hThi = keep("hThi", [P, KT, T], F32R, c)
            hTlo = keep("hTlo", [P, KT, T], F32R, c)
        with ExitStack() as c:
            vin = keep("v_in", [P, 2, TT, P], where=c)
            qT = keep("qT", [P, 2, T], where=c)
            kT = keep("kT", [P, 2, T], where=c)
            bias = keep("bias", [P, 2, 2, BAND], where=c)
            S = keep("S", [P, 2, BAND], where=c)
            Pr = keep("Pr", [P, 2, BAND], where=c)
            PT = keep("PT", [P, 2, BAND], where=c)
            nmax = keep("nmax", [P, 2, TT], where=c)
            psumr = keep("psumr", [P, 2, 2, TT], where=c)
            rcp = keep("rcp", [P, 2, TT], where=c)
        with ExitStack() as c:
            hidhi = keep("hidhi", [P, 2, 2, T], F32R, c, "right")
            hidlo = keep("hidlo", [P, 2, 2, T], F32R, c, "right")
            sil = keep("sil", [P, 2, HALF], where=c, side="right")
            prod = keep("prod", [P, 2, HALF], where=c, side="right")
        with ExitStack() as c:
            fF = keep("fF", [P, T], where=c, side="right")
            fQ = keep("fQ", [P, T], where=c, side="right")
            hK = keep("hK", [P, T], where=c, side="right")
            hQ = keep("hQ", [P, T], where=c, side="right")
            hV = keep("hV", [P, TT, P], where=c, side="right")
            hG = keep("hG", [P, TT, P], where=c, side="right")
            tot = keep("tot", [P, T], where=c, side="right")
            aT = keep("aT", [P, T], where=c, side="right")
            kS = keep("kS", [P, TT, P], where=c, side="right")
            st = keep("st", [P, TT, P], where=c, side="right")
            mk = keep("mk", [P, (LEVELS - 1) * HALF], U8, c, "right")
            sso = keep("sso", [P, TT], where=c, side="right")
            rso = keep("rso", [P, TT], where=c, side="right")
        with ExitStack() as c:
            cat = keep("cat", [P, TT, D], where=c, side="right")

        qin = y[:, 1, :].rearrange("p (t c) -> p t c", t=TT)
        kin = gain[:, :].rearrange("p (t c) -> p t c", t=TT)
        relrow = aT[0:AH, 0:N_REL]
        extrow = kS[0:AH, :, :].rearrange("p a b -> p (a b)")[:, 0:EXT]

        ps = ctx.enter_context(nc.psum_tensor("ps", [P, 8 * HALF], F32))

        def bank(b, n=HALF):
            return ps[:, b * HALF:b * HALF + n]

        x_loaded = [sem(f"x_loaded{t}") for t in range(TT)]
        ident_loaded = sem("ident_loaded")
        lb_loaded = sem("lb_loaded")
        gn_loaded = sem("gn_loaded")
        gain_loaded = sem("gain_loaded")
        mhalf_set = sem("mhalf_set")
        raw_loaded = [sem(f"raw_loaded{s}") for s in range(RING)]
        split_hi = sem("split_hi")
        split_lo = sem("split_lo")
        piece_used = sem("piece_used")
        ss_ready = sem("ss_ready")
        var_ready = sem("var_ready")
        rstd_ready = sem("rstd_ready")
        y_ready = sem("y_ready")
        turned = sem("turned")
        hT_hi_ready = sem("hT_hi_ready")
        hT_ready = sem("hT_ready")
        gate_done = sem("gate_done")
        up_done = sem("up_done")
        silu_done = sem("silu_done")
        prod_done = sem("prod_done")
        hid_hi_ready = sem("hid_hi_ready")
        hid_ready = sem("hid_ready")
        row_done = sem("row_done")
        x_added = sem("x_added")
        out_stored = sem("out_stored")
        proj_done = sem("proj_done")
        proj_evac = sem("proj_evac")
        proj_stored = [sem(f"proj_stored{s}") for s in range(2)]
        lb_diff = sem("lb_diff")
        lb_sig = sem("lb_sig")
        lb_ready = sem("lb_ready")
        sig_ready = sem("sig_ready")
        mask_loaded = sem("mask_loaded")
        mask_set = sem("mask_set")
        fq_loaded = sem("fq_loaded")
        v_loaded = sem("v_loaded")
        g_loaded = sem("g_loaded")
        hgrn_step = sem("hgrn_step")
        scaled = sem("scaled")
        scores_done = sem("scores_done")
        scores_kept = sem("scores_kept")
        k_turned = sem("k_turned")
        k_rows = sem("k_rows")
        outer_done = sem("outer_done")
        state_step = sem("state_step")
        read_done = sem("read_done")
        read_sq = sem("read_sq")
        read_ss = sem("read_ss")
        read_var = sem("read_var")
        read_rstd = sem("read_rstd")
        gate_gained = sem("gate_gained")
        ro_ready = sem("ro_ready")
        ro_stored = sem("ro_stored")
        rel_loaded = sem("rel_loaded")
        ext_step = sem("ext_step")
        ext_stored = sem("ext_stored")
        bias_stored = sem("bias_stored")
        qk_gain_loaded = sem("qk_gain_loaded")
        qk_gain_ready = sem("qk_gain_ready")
        qk_loaded = [sem(f"{w}_loaded") for w in "qk"]
        av_loaded = [sem(f"av_loaded{p}") for p in range(2)]
        bias_loaded = sem("bias_loaded")
        bias_masked = sem("bias_masked")
        qk_sq = sem("qk_sq")
        qk_ss = sem("qk_ss")
        qk_var = sem("qk_var")
        qk_rstd = sem("qk_rstd")
        qk_normed = sem("qk_normed")
        qk_turned = sem("qk_turned")
        qkT_ready = sem("qkT_ready")
        unit_scores = sem("unit_scores")
        unit_max = sem("unit_max")
        unit_exp = sem("unit_exp")
        unit_turned = sem("unit_turned")
        PT_by_vector = sem("PT_by_vector")
        PT_by_scalar = sem("PT_by_scalar")
        unit_out = sem("unit_out")
        rcp_ready = sem("rcp_ready")
        head_out = sem("head_out")
        cat_loaded = sem("cat_loaded")
        dve_passed = sem("dve_passed")
        pool_passed = sem("pool_passed")

        block = ctx.enter_context(nc.Block())

        def wait_PT(eng, v, i):
            if by_scalar(v):
                eng.wait_ge(PT_by_scalar, (v + 1) // 3 + 8 * i)
            else:
                eng.wait_ge(PT_by_vector, v + 1 - (v + 1) // 3 + 16 * i)

        def norm_no(R):
            return R if R < R_CAT else 2

        @block.sync
        def _(sp):
            def piece(n0, adv, src, shape):
                if n0 >= RING:
                    sp.wait_ge(split_lo, n0 - RING + 1 + adv)
                dst = raw[:, n0 % RING, :]
                if shape:
                    dst = dst.rearrange("p (k c) -> p k c", k=shape)
                sp.dma_start(dst, src).then_inc(raw_loaded[n0 % RING], 16)

            def ffn(base, w_gate, w_up, w_down):
                wg = w_gate[0].rearrange("(k p) f -> p k f", p=P)
                wu = w_up[0].rearrange("(k p) f -> p k f", p=P)

                def gate_up(f, n0, adv):
                    piece(n0, adv, wg[:, :, ds(f * P, P)], KT)
                    piece(n0 + 1, adv, wu[:, :, ds(f * P, P)], KT)

                def down(f, n0, adv):
                    piece(n0, adv, w_down[0][ds(f * P, P), :], 0)

                gate_up(0, base, 0)
                gate_up(1, base + 2, 0)
                with sp.Fori(0, NG // 2) as i:
                    for g in range(2):
                        n0 = base + 4 + 6 * g
                        gate_up(4 * i + 2 + 2 * g, n0, 12 * i)
                        gate_up(4 * i + 3 + 2 * g, n0 + 2, 12 * i)
                        down(4 * i + 2 * g, n0 + 4, 12 * i)
                        down(4 * i + 2 * g + 1, n0 + 5, 12 * i)
                down(FT - 2, base + PIECES_FFN - 2, 0)
                down(FT - 1, base + PIECES_FFN - 1, 0)

            sp.dma_start(xs[:, 0, :], x[0, 0:P, :]).then_inc(x_loaded[0], 16)
            ffn(P_FFN1, ffn1_w_gate, ffn1_w_up, ffn1_w_down)

            wi = w_in[0].rearrange("(q k p) c -> q p k c", p=P, k=2)

            def mix_group(col, n0, adv):
                for q in range(4):
                    piece(n0 + q, adv, wi[q][:, :, ds(col, HALF)], 2)

            with sp.Fori(0, 4) as n:
                mix_group(HALF * n + 3 * HALF, P_MIX, 4 * n)
            with sp.Fori(0, 3) as n:
                mix_group(HALF * n, P_MIX + 16, 4 * n)
            wo = w_out[0].rearrange("(q k p) c -> q p k c", p=P, k=2)
            for h in range(2):
                for q in range(4):
                    piece(P_OUT + 4 * h + q, 0, wo[q][:, :, h * HALF:(h + 1) * HALF], 2)
            ffn(P_FFN2, ffn2_w_gate, ffn2_w_up, ffn2_w_down)

        @block.tensor
        def _(pe):
            def three(dst, a, b, first, last):
                (ahi, alo), (bhi, blo) = a, b
                pe.matmul(dst, ahi, bhi, start=first, stop=False)
                pe.matmul(dst, ahi, blo, start=False, stop=False)
                return pe.matmul(dst, alo, bhi, start=False, stop=last)

            def turn_tile(R, t):
                r = TT * R + t
                if R == R_CAT:
                    if t == 0:
                        pe.wait_ge(head_out, AH)
                        pe.wait_ge(cat_loaded, 16)
                    src = cat[:, t, :]
                else:
                    q = TT * norm_no(R) + t
                    pe.wait_ge(y_ready, q + 1)
                    src = y[:, t % 2, :]
                if r >= 2:
                    pe.wait_ge(hT_ready, r - 1)
                if t < 2 and R == R_MIX:
                    pe.wait_ge(prod_done, 2 * FT)
                c0 = turn_bank(R, t) * HALF
                for k in range(KT):
                    mm = pe.transpose(ps[:, c0 + k * P:c0 + (k + 1) * P],
                                      src[:, k * P:(k + 1) * P], ident[:, :])
                mm.then_inc(turned, 1)

            def ffn(F, base, adds, R):
                e_base = 2 * FT * F

                def product(which, h, f0, advf, n0, adv):
                    s = (n0 + which) % RING
                    e = e_base + 2 * f0 + h
                    pe.wait_ge(split_lo, n0 + which + 1 + adv)
                    if f0 and which == 0:
                        pe.wait_ge(silu_done, e - 1 + 2 * advf)
                    elif f0:
                        pe.wait_ge(prod_done, e - 1 + 2 * advf)
                    for k in range(KT):
                        mm = three(bank(2 * which + h),
                                   [w[:, s, k * P:(k + 1) * P] for w in (whi, wlo)],
                                   [a[:, k, h * HALF:(h + 1) * HALF] for a in (hThi, hTlo)],
                                   k == 0, k == KT - 1)
                    mm.then_inc((gate_done, up_done)[which], 1)

                def gate_up(f0, advf, n0, adv):
                    for which in range(2):
                        for h in range(2):
                            product(which, h, f0, advf, n0, adv)

                def first_tile():
                    r = TT * R
                    if R == R_FFN1:
                        pe.wait_ge(hT_ready, r + 4)
                        product(0, 0, 0, 0, base, 0)
                        turn_tile(R, 4)
                        turn_tile(R, 5)
                        product(1, 0, 0, 0, base, 0)
                        turn_tile(R, 6)
                        turn_tile(R, 7)
                    else:
                        pe.wait_ge(hT_ready, r + 6)
                        product(0, 0, 0, 0, base, 0)
                        turn_tile(R, 7)
                        pe.wait_ge(hT_ready, r + 7)
                        product(1, 0, 0, 0, base, 0)
                    pe.wait_ge(hT_ready, r + 8)
                    product(0, 1, 0, 0, base, 0)
                    product(1, 1, 0, 0, base, 0)

                def down(g0, advg, n0, adv, tail=None):
                    par = g0 % 2
                    pe.wait_ge(split_lo, n0 + 2 + adv)
                    pe.wait_ge(hid_ready, e_base + 4 * g0 + 4 + 4 * advg)
                    for t in range(TT):
                        for h in range(2):
                            d = adds + 16 * g0 + 2 * t + h
                            if d >= 4:
                                pe.wait_ge(x_added, d - 3 + 16 * advg)
                            for j in range(2):
                                s = (n0 + j) % RING
                                mm = three(bank(4 + d % 4),
                                           [a[:, par, j, t * P:(t + 1) * P] for a in (hidhi, hidlo)],
                                           [w[:, s, h * HALF:(h + 1) * HALF] for w in (whi, wlo)],
                                           j == 0, j == 1)
                            mm.then_inc(row_done, 1)
                        if tail is not None and t >= 2:
                            turn_tile(tail, t - 2)

                first_tile()
                gate_up(1, 0, base + 2, 0)
                with pe.Fori(0, NG // 2) as i:
                    for g in range(2):
                        n0 = base + 4 + 6 * g
                        gate_up(2 + 2 * g, 4 * i, n0, 12 * i)
                        gate_up(3 + 2 * g, 4 * i, n0 + 2, 12 * i)
                        down(g, 2 * i, n0 + 4, 12 * i)
                down(NG - 1, 0, base + PIECES_FFN - 2, 0, tail=R_MIX if F == 0 else None)

            pe.wait_ge(ident_loaded, 16)
            for t in range(4):
                turn_tile(R_FFN1, t)
            ffn(0, P_FFN1, A_FFN1, R_FFN1)

            def group(n0, advn, feature, hook):
                base = P_MIX + 4 * n0
                for o in range(8):
                    idx = 8 * n0 + o
                    if idx >= 4:
                        pe.wait_ge(proj_evac, idx - 3 + 8 * advn)
                    else:
                        pe.wait_ge(x_added, A_OUT)
                    if n0 == 0:
                        pe.wait_ge(hT_ready, TT * R_MIX + (4 if o < 2 else 8))
                    for k in range(KT):
                        s = (base + k // 2) % RING
                        if o == 0 and k % 2 == 0:
                            pe.wait_ge(split_lo, base + k // 2 + 1 + 4 * advn)
                        c0 = (k % 2) * HALF
                        if feature:
                            f, h = FEATURE_ORDER[o]
                            a = [w[:, s, c0 + f * P:c0 + (f + 1) * P] for w in (whi, wlo)]
                            b = [v[:, k, h * HALF:(h + 1) * HALF] for v in (hThi, hTlo)]
                        else:
                            a = [v[:, k, o * P:(o + 1) * P] for v in (hThi, hTlo)]
                            b = [w[:, s, c0:c0 + HALF] for w in (whi, wlo)]
                        mm = three(bank(4 + o % 4), a, b, k == 0, k == KT - 1)
                        if o == 7 and k % 2 == 1 and k < KT - 1:
                            mm.then_inc(piece_used, 1)
                        if k == 3:
                            hook(2 * o)
                    mm.then_inc(proj_done, 1)
                    hook(2 * o + 1)

            def hgrn(j):
                def hook(at):
                    if at in LEVEL_AT:
                        L = LEVEL_AT[at]
                        pe.wait_ge(scaled, 9 * j + L + 1)
                        if L == 0:
                            pe.wait_ge(ro_ready, j + 1)
                            for c in range(TT):
                                mm = pe.matmul(ps[:, c * P:(c + 1) * P], hK[:, c * P:(c + 1) * P],
                                               fQ[:, c * P:(c + 1) * P], start=True, stop=True)
                        else:
                            h = 1 << (L - 1)
                            if L >= 3:
                                pe.wait_ge(scores_kept, 8 * j + L - 1)
                            b = 2 + L % 2
                            q = hQ[:, :].rearrange("p (c b two h) -> p c b two h", c=TT, two=2, h=h)
                            for c in range(TT):
                                mm = pe.matmul(
                                    ps[:, b * HALF + c * 64:b * HALF + (c + 1) * 64],
                                    hK[:, c * P:(c + 1) * P], q[:, c, :, 1, :], start=True, stop=True)
                        mm.then_inc(scores_done, 1)
                    elif at == TURN_AT:
                        pe.wait_ge(scaled, 9 * j + 9)
                        for c in range(TT):
                            mm = pe.transpose(ps[:, c * P:(c + 1) * P], hK[:, c * P:(c + 1) * P], ident[:, :])
                        mm.then_inc(k_turned, 1)
                    elif at == OUTER_AT:
                        pe.wait_ge(k_rows, j + 1)
                        pe.wait_ge(v_loaded, 16 * j + 16)
                        pe.wait_ge(scores_kept, 8 * j + 8)
                        for c in range(TT - 1):
                            mm = pe.matmul(ps[:, 2 * HALF + c * P:2 * HALF + (c + 1) * P],
                                           kS[:, c, :], hV[:, c, :], start=True, stop=True)
                        mm.then_inc(outer_done, 1)
                    elif at == READ_AT:
                        pe.wait_ge(state_step, 7 * j + 7)
                        for c in range(TT):
                            dst = ps[:, c * P:(c + 1) * P]
                            mm = pe.matmul(dst, aT[:, c * P:(c + 1) * P], hV[:, c, :],
                                           start=True, stop=(c == 0))
                            if c:
                                mm = pe.matmul(dst, hQ[:, c * P:(c + 1) * P], st[:, c, :],
                                               start=False, stop=True)
                        mm.then_inc(read_done, 1)
                return hook

            def nothing(at):
                return None

            def last_turns(at):
                if at == 1:
                    turn_tile(R_MIX, TT - 2)
                    turn_tile(R_MIX, TT - 1)

            group(0, 0, True, last_turns)
            group(1, 0, True, nothing)
            group(2, 0, False, nothing)
            pe.nop().then_inc(k_turned, 1)
            pe.nop().then_inc(read_done, 1)
            with pe.Fori(0, HH) as j:
                group(3, j, False, hgrn(j))

            def turn_qk(pp, w, b, i):
                pe.wait_ge(qk_normed, 2 * pp + w + 1 + 4 * i)
                for t in range(TT):
                    mm = pe.transpose(ps[:, b * HALF + t * P:b * HALF + (t + 1) * P],
                                      (qin, kin)[w][:, t, :], ident[:, :])
                mm.then_inc(qk_turned, 1)

            def two_pairs(i):
                def scores(v):
                    pp, hd, parts = unit(v)
                    if v >= 2:
                        pe.wait_ge(unit_max, v - 1 + NU * 2 * i)
                    if v in (0, NU):
                        pe.wait_ge(qkT_ready, 2 * pp + 2 + 4 * i)
                    rows = slice(hd * DH, (hd + 1) * DH)
                    b = 2 * (v % 2) * HALF
                    for t, n, c0 in parts:
                        lo = (t - n + 1) * P
                        for c, m in ((c0, min(n * P, HALF - c0)), (HALF, c0 + n * P - HALF)):
                            if c >= c0 and m > 0:
                                mm = pe.matmul(ps[:, b + c:b + c + m], qT[rows, pp, t * P:(t + 1) * P],
                                               kT[rows, pp, lo + c - c0:lo + c - c0 + m],
                                               start=True, stop=True)
                    mm.then_inc(unit_scores, 1)

                def turn(v):
                    pe.wait_ge(unit_exp, v + 1 + NU * 2 * i)
                    if v >= 1:
                        wait_PT(pe, v - 1, i)
                    if v - 1 in TURN_QK_AT:
                        pe.wait_ge(qkT_ready, TURN_QK_AT.index(v - 1) + 3 + 4 * i)
                    for c in range(KEY_TILES):
                        mm = pe.transpose(ps[:, 4 * HALF + c * P:4 * HALF + (c + 1) * P],
                                          Pr[:, v % 2, c * P:(c + 1) * P], ident[:, :])
                    mm.then_inc(unit_turned, 1)

                def values(v):
                    pp, hd, parts = unit(v)
                    wait_PT(pe, v, i)
                    if v in (0, NU):
                        pe.wait_ge(av_loaded[pp], 16 + 16 * i)
                    if v in (NU, NU + 1):
                        pe.wait_ge(head_out, hd + 1 + 4 * i)
                    for t, n, c0 in parts:
                        dst = ps[:, (6 + hd) * HALF + t * DH:(6 + hd) * HALF + (t + 1) * DH]
                        for c in range(n):
                            mm = pe.matmul(dst, PT[:, v % 2, c0 + c * P:c0 + (c + 1) * P],
                                           vin[:, pp, t - n + 1 + c, hd * DH:(hd + 1) * DH],
                                           start=(c == 0), stop=(c == n - 1))
                    mm.then_inc(unit_out, 1)

                turn_qk(0, 0, 0, i)
                turn_qk(0, 1, 2, i)
                for v in range(2 * NU + 2):
                    if v < 2 * NU:
                        scores(v)
                    if 1 <= v <= 2 * NU:
                        turn(v - 1)
                    if v - 1 in TURN_QK_AT:
                        wait_PT(pe, v - 1, i)
                        turn_qk(1, TURN_QK_AT.index(v - 1), 4, i)
                    if v >= 2:
                        values(v - 2)

            pe.wait_ge(proj_evac, 56)
            pe.wait_ge(ro_ready, HH + 1)
            with pe.Fori(0, 2) as i:
                two_pairs(i)

            turn_tile(R_CAT, 0)
            turn_tile(R_CAT, 1)
            for h in range(2):
                for t in range(TT):
                    d = A_OUT + 8 * h + t
                    if h == 0:
                        pe.wait_ge(hT_ready, TT * R_CAT + t + 1)
                    if 8 * h + t >= 4:
                        pe.wait_ge(x_added, d - 3)
                    for k in range(KT):
                        s = (P_OUT + 4 * h + k // 2) % RING
                        if t == 0 and k % 2 == 0:
                            pe.wait_ge(split_lo, P_OUT + 4 * h + k // 2 + 1)
                        c0 = (k % 2) * HALF
                        mm = three(bank(4 + d % 4), [a[:, k, t * P:(t + 1) * P] for a in (hThi, hTlo)],
                                   [w[:, s, c0:c0 + HALF] for w in (whi, wlo)], k == 0, k == KT - 1)
                        if t == TT - 1 and k % 2 == 1 and k < KT - 1:
                            mm.then_inc(piece_used, 1)
                    mm.then_inc(row_done, 1)
                    if h == 0 and t + 2 < TT:
                        turn_tile(R_CAT, t + 2)
                    if h == 1 and t >= 1:
                        turn_tile(R_FFN2, t - 1)
            ffn(1, P_FFN2, A_FFN2, R_FFN2)

        @block.scalar
        def _(act):
            def split(n0, adv=0):
                s = n0 % RING
                act.wait_ge(raw_loaded[s], 16 * (n0 // RING + 1) + 4 * adv)
                act.activation(whi[:, s, :], raw[:, s, :], ACT.Copy).then_inc(split_hi, 1)

            def square(R, t):
                q = TT * norm_no(R) + t
                if R == R_FFN1:
                    act.wait_ge(x_loaded[t], 16)
                elif R == R_MIX:
                    act.wait_ge(x_added, A_FFN1 + ADDS_FFN - 16 + 2 * t + 2)
                else:
                    act.wait_ge(x_added, A_OUT + 8 + t + 1)
                if q:
                    act.wait_ge(ss_ready, q)
                if R == R_FFN2 and t == 0:
                    act.wait_ge(qk_ss, AH + 1)
                act.activation(junk[:, :], xs[:, t, :], ACT.Square,
                               accum_out=ss[:, q:q + 1]).then_inc(ss_ready, 1)

            def hT_hi(R, t):
                r = TT * R + t
                act.wait_ge(turned, r + 1)
                c0 = turn_bank(R, t) * HALF
                src = ps[:, c0:c0 + D].rearrange("p (k c) -> p k c", k=KT)
                act.activation(hThi[:, :, t * P:(t + 1) * P], src, ACT.Copy).then_inc(hT_hi_ready, 1)

            def used(group, q, advn=0):
                if q < 3:
                    act.wait_ge(piece_used, 3 * group + q + 1 + 3 * advn)
                elif group < 7:
                    act.wait_ge(proj_done, 8 * group + 8 + 8 * advn)
                else:
                    act.wait_ge(row_done, A_OUT + 8 * (group - 7) + 8)

            def ffn(F, base, adds, tail):
                e_base = 2 * FT * F

                def tile(f0, advf, n0, adv):
                    for h in range(2):
                        e = e_base + 2 * f0 + h
                        act.wait_ge(gate_done, e + 1 + 2 * advf)
                        if e >= 2:
                            act.wait_ge(prod_done, e - 1 + 2 * advf)
                        act.activation(sil[:, h, :], bank(h), ACT.Silu).then_inc(silu_done, 1)
                        if h == 0:
                            split(n0 + 2, adv)
                    split(n0 + 3, adv)
                    for h in range(2):
                        e = e_base + 2 * f0 + h
                        act.wait_ge(prod_done, e + 1 + 2 * advf)
                        act.activation(hidhi[:, (f0 // 2) % 2, f0 % 2, h * HALF:(h + 1) * HALF],
                                       prod[:, h, :], ACT.Copy).then_inc(hid_hi_ready, 1)

                tile(0, 0, base, 0)
                tile(1, 0, base + 2, 0)
                with act.Fori(0, NG // 2) as i:
                    for g in range(2):
                        n0 = base + 4 + 6 * g
                        tile(2 + 2 * g, 4 * i, n0, 12 * i)
                        tile(3 + 2 * g, 4 * i, n0 + 2, 12 * i)
                        last = g == 1
                        split(n0 + 6, 12 * i)
                        split(n0 + 7, 12 * i)
                if tail:
                    act.wait_ge(row_done, adds + 16 * (NG - 1))
                    split(base + PIECES_FFN)
                    split(base + PIECES_FFN + 1)
                    for t in range(TT + 2):
                        if t < TT:
                            square(R_MIX, t)
                        if t == TT:
                            act.wait_ge(row_done, A_OUT)
                            split(P_MIX + 2)
                            split(P_MIX + 3)
                        if t >= 2:
                            hT_hi(R_MIX, t - 2)

            act.dma_start(ident[:, :], identity).then_inc(ident_loaded, 16)
            for t in range(1, TT):
                act.dma_start(xs[:, t, :], x[0, t * P:(t + 1) * P, :]).then_inc(x_loaded[t], 16)
            for t in range(TT + 2):
                if t < TT:
                    square(R_FFN1, t)
                if t >= 2:
                    hT_hi(R_FFN1, t - 2)
                if t == 3:
                    split(0)
                if t == 5:
                    split(1)
            ffn(0, P_FFN1, A_FFN1, True)

            def stage(o):
                return y[:, 0, (o % 2) * HALF:(o % 2 + 1) * HALF]

            def evac(n0, advn, o, func):
                idx = 8 * n0 + o
                act.wait_ge(proj_done, idx + 1 + 8 * advn)
                if idx >= 2:
                    act.wait_ge(proj_stored[o % 2], 16 * (idx // 2) + 64 * advn)
                if func == ACT.Sigmoid:
                    act.activation(stage(o), bank(4 + o % 4), ACT.Sigmoid).then_inc(sig_ready, 1)
                    act.wait_ge(sig_ready, o + 1)
                    f = FEATURE_ORDER[o][0]
                    act.activation(stage(o), stage(o), ACT.Identity, scale=lb[:, 1, f:f + 1],
                                   bias=lb[:, 0, f:f + 1]).then_inc(proj_evac, 1)
                else:
                    act.activation(stage(o), bank(4 + o % 4), func).then_inc(proj_evac, 1)

            def store(n0, advn, o, feature):
                idx = 8 * n0 + o
                act.wait_ge(proj_evac, idx + 1 + 8 * advn)
                if feature:
                    f, h = FEATURE_ORDER[o]
                    row = n0 * HALF + f * P
                    dst = feat[row:row + P, h * HALF:(h + 1) * HALF]
                else:
                    dst = tok[o * P:(o + 1) * P, ds(n0 - 2 + advn, 1), :].rearrange("p a c -> p (a c)")
                act.dma_start(dst, stage(o)).then_inc(proj_stored[o % 2], 16)

            def group(n0, advn, func, feature=False, head=None):
                for o in range(7):
                    evac(n0, advn, o, func)
                    store(n0, advn, o, feature)
                if head is not None:
                    act.wait_ge(k_turned, head + 2)
                    act.activation(kS[:, :, :].rearrange("p a b -> p (a b)"), ps[:, 0:1024], ACT.Copy)\
                       .then_inc(k_rows, 1)
                for q in range(4):
                    used(n0, q, advn)
                    split(P_MIX + 4 * n0 + 4 + q, 4 * advn)
                evac(n0, advn, 7, func)
                store(n0, advn, 7, feature)
                if head is not None:
                    act.wait_ge(read_done, head + 2)
                    act.wait_ge(read_ss, head + 1)
                    act.wait_ge(ss_ready, 2 * TT)
                    act.activation(junk[:, :], ps[:, 0:1024], ACT.Square).then_inc(read_sq, 1)

            group(0, 0, ACT.Silu, True)
            act.wait_ge(lb_diff, 1)
            act.activation(lb[:, 0, :], lb[:, 2, :], ACT.Sigmoid).then_inc(lb_sig, 1)
            act.wait_ge(lb_ready, 1)
            group(1, 0, ACT.Sigmoid, True)
            group(2, 0, ACT.Copy)
            group(3, 0, ACT.Silu, head=0)
            with act.Fori(1, HH) as j:
                group(3, j, ACT.Copy, head=j)

            def square_qk(pp, w, i):
                act.wait_ge(qk_loaded[w], 16 * pp + 16 + 32 * i)
                act.wait_ge(qk_ss, 2 * pp + w + 1 + 4 * i)
                act.activation(junk[:, :], (qin, kin)[w].rearrange("p a b -> p (a b)"),
                               ACT.Square).then_inc(qk_sq, 1)

            def take_qk(pp, w, b, i):
                act.wait_ge(qk_turned, 2 * pp + w + 1 + 4 * i)
                act.activation((qT, kT)[w][:, pp, :], ps[:, b * HALF:b * HALF + T], ACT.Copy,
                               scale=qkg[:, w:w + 1]).then_inc(qkT_ready, 1)

            def two_pairs(i):
                square_qk(0, 0, i)
                square_qk(0, 1, i)
                take_qk(0, 0, 0, i)
                take_qk(0, 1, 2, i)
                for v in range(2 * NU + 1):
                    if v < 2 * NU:
                        pp, hd, parts = unit(v)
                        act.wait_ge(unit_max, v + 1 + 2 * NU * i)
                        if v >= 2:
                            act.wait_ge(unit_turned, v - 1 + 2 * NU * i)
                        for t, n, c0 in parts:
                            last = act.activation(Pr[:, v % 2, c0:c0 + n * P], S[:, v % 2, c0:c0 + n * P],
                                                  ACT.Exp, scale=-1.0, bias=nmax[:, hd, t:t + 1],
                                                  accum_out=psumr[:, pp, hd, t:t + 1])
                        last.then_inc(unit_exp, 1)
                    if v >= 1 and by_scalar(v - 1):
                        act.wait_ge(unit_turned, v + 2 * NU * i)
                        if v >= 3:
                            act.wait_ge(unit_out, v - 2 + 2 * NU * i)
                        act.activation(PT[:, (v - 1) % 2, :], ps[:, 4 * HALF:4 * HALF + BAND], ACT.Copy)\
                           .then_inc(PT_by_scalar, 1)
                    if v in SQUARE_AT:
                        square_qk(1, SQUARE_AT.index(v), i)
                    if v - 1 in TURN_QK_AT:
                        take_qk(1, TURN_QK_AT.index(v - 1), 4, i)

            with act.Fori(0, 2) as i:
                two_pairs(i)

            for t in range(TT):
                hT_hi(R_CAT, t)
            for q in range(4):
                used(7, q)
                split(P_OUT + 4 + q)
            for t in range(TT + 1):
                if t == TT - 1:
                    for q in range(2):
                        used(8, q)
                        split(P_FFN2 + q)
                if t < TT:
                    square(R_FFN2, t)
                if t >= 1:
                    hT_hi(R_FFN2, t - 1)
            ffn(1, P_FFN2, A_FFN2, False)
            for t in range(TT):
                act.wait_ge(x_added, A_FFN2 + ADDS_FFN - 16 + 2 * t + 2)
                act.dma_start(out[0, t * P:(t + 1) * P, :], xs[:, t, :]).then_inc(out_stored, 16)
            act.wait_ge(out_stored, 16 * TT)

        @block.vector
        def _(dve):
            def split(n0, adv=0):
                s = n0 % RING
                dve.wait_ge(split_hi, n0 + 1 + adv)
                dve.tensor_tensor(wlo[:, s, :], raw[:, s, :], whi[:, s, :].bitcast(F32), ALU.subtract)\
                   .then_inc(split_lo, 1)

            def normalise(R, t):
                q = TT * norm_no(R) + t
                dve.wait_ge(rstd_ready, q + 1)
                if t == 0:
                    dve.wait_ge(gain_loaded, 16 * norm_no(R) + 16)
                if t >= 2:
                    dve.wait_ge(turned, TT * R + t - 1)
                dve.scalar_tensor_tensor(y[:, t % 2, :], xs[:, t, :], rstd[:, q:q + 1], gain[:, :],
                                         ALU.mult, ALU.mult).then_inc(y_ready, 1)

            def hT_lo(R, t):
                r = TT * R + t
                dve.wait_ge(hT_hi_ready, r + 1)
                c0 = turn_bank(R, t) * HALF
                src = ps[:, c0:c0 + D].rearrange("p (k c) -> p k c", k=KT)
                dve.tensor_tensor(hTlo[:, :, t * P:(t + 1) * P], src,
                                  hThi[:, :, t * P:(t + 1) * P].bitcast(F32), ALU.subtract)\
                   .then_inc(hT_ready, 1)

            def add(d0, advd, t, h, scale):
                dve.wait_ge(row_done, d0 + 1 + advd)
                dst = xs[:, t, h * HALF:(h + 1) * HALF]
                dve.scalar_tensor_tensor(dst, bank(4 + d0 % 4), scale, dst, ALU.mult, ALU.add)\
                   .then_inc(x_added, 1)

            def ffn(F, base, adds, tail):
                e_base = 2 * FT * F

                def tile(f0, advf, n0, adv):
                    split(n0 + 2, adv)
                    split(n0 + 3, adv)
                    for h in range(2):
                        e = e_base + 2 * f0 + h
                        dve.wait_ge(silu_done, e + 1 + 2 * advf)
                        dve.wait_ge(up_done, e + 1 + 2 * advf)
                        if e >= 2:
                            dve.wait_ge(hid_ready, e - 1 + 2 * advf)
                        dve.tensor_tensor(prod[:, h, :], bank(2 + h), sil[:, h, :], ALU.mult)\
                           .then_inc(prod_done, 1)
                    for h in range(2):
                        e = e_base + 2 * f0 + h
                        dve.wait_ge(hid_hi_ready, e + 1 + 2 * advf)
                        at = (slice(None), (f0 // 2) % 2, f0 % 2, slice(h * HALF, (h + 1) * HALF))
                        dve.tensor_tensor(hidlo[at], prod[:, h, :], hidhi[at].bitcast(F32), ALU.subtract)\
                           .then_inc(hid_ready, 1)

                tile(0, 0, base, 0)
                tile(1, 0, base + 2, 0)
                with dve.Fori(0, NG // 2) as i:
                    for g in range(2):
                        n0 = base + 4 + 6 * g
                        tile(2 + 2 * g, 4 * i, n0, 12 * i)
                        tile(3 + 2 * g, 4 * i, n0 + 2, 12 * i)
                        for t in range(TT):
                            for h in range(2):
                                add(adds + 16 * g + 2 * t + h, 32 * i, t, h, 0.5)
                            if t in (1, 3):
                                split(n0 + 6 + t // 2, 12 * i)
                d0 = adds + 16 * (NG - 1)
                if tail:
                    split(base + PIECES_FFN)
                    split(base + PIECES_FFN + 1)
                for t in range(TT):
                    for h in range(2):
                        add(d0 + 2 * t + h, 0, t, h, 0.5)
                    if tail:
                        if t >= 1:
                            normalise(R_MIX, t - 1)
                        if t >= 2:
                            hT_lo(R_MIX, t - 2)
                if tail:
                    normalise(R_MIX, TT - 1)
                    split(P_MIX + 2)
                    split(P_MIX + 3)
                    hT_lo(R_MIX, TT - 2)
                    hT_lo(R_MIX, TT - 1)

            for t in range(TT + 2):
                if t < TT:
                    normalise(R_FFN1, t)
                if t >= 2:
                    hT_lo(R_FFN1, t - 2)
                if t == 5:
                    split(0)
                if t == 7:
                    split(1)
            ffn(0, P_FFN1, A_FFN1, True)

            dve.wait_ge(lb_loaded, 16)
            dve.tensor_tensor(lb[:, 2, :], lbs[:, 0, :], lbs[:, 1, :], ALU.subtract).then_inc(lb_diff, 1)
            dve.wait_ge(mask_loaded, 16)
            for L in range(LEVELS - 1):
                m = bass.AP(tot, L * 64, [list(tot[:, :].ap[0]), [0, TT], [1, 64]])
                dve.tensor_copy(mk[:, L * HALF:(L + 1) * HALF].rearrange("p (c t) -> p c t", c=TT), m)\
                   .then_inc(mask_set, 1)
            dve.wait_ge(rel_loaded, 16)
            n_far = EXT - 1 - (REL_CLIP + 127)
            dve.tensor_copy(extrow[:, n_far:EXT - 1], relrow[:, N_REL - 2:0:-1]).then_inc(ext_step, 1)
            dve.tensor_copy(extrow[:, 0:n_far], relrow[:, N_REL - 1:N_REL].to_broadcast([AH, n_far]))\
               .then_inc(ext_step, 1)
            dve.memset(extrow[:, EXT - 1:EXT], 0.0).then_inc(ext_step, 1)
            dve.wait_ge(qk_gain_loaded, 64)
            dve.tensor_scalar(qkg[:, 0:1], qkg[:, 0:1], DH ** -0.5, None, ALU.mult).then_inc(qk_gain_ready, 1)
            for q in range(4):
                split(P_MIX + 4 + q)
            dve.wait_ge(lb_sig, 1)
            dve.tensor_scalar(lb[:, 1, :], lb[:, 0, :], -1.0, 1.0, ALU.mult, ALU.add).then_inc(lb_ready, 1)
            for n in (1, 2):
                for q in range(4):
                    split(P_MIX + 4 * n + 4 + q)

            def head(j):
                n = [0]

                def link(ins):
                    n[0] += 1
                    ins.then_inc(hgrn_step, 1)
                    dve.wait_ge(hgrn_step, n[0] + per_head * j)

                def keep_scores(L):
                    if L:
                        dve.wait_ge(mask_set, LEVELS - 1)
                    dve.wait_ge(scores_done, 8 * j + L + 1)
                    if L == 0:
                        dst = aT[:, :].rearrange("p (c t) -> p c t", c=TT)
                        src = ps[:, 0:1024].rearrange("p (c t) -> p c t", c=TT)
                        eye = bass.AP(ident, 0, [list(ident[:, :].ap[0]), [0, TT], [1, P]])
                        dve.tensor_tensor(dst, src, eye, ALU.mult).then_inc(scores_kept, 1)
                        return
                    dve.wait_ge(scores_kept, 8 * j + L)
                    h = 1 << (L - 1)
                    dst = aT[:, :].rearrange("p (b two h) -> p b two h", two=2, h=h)[:, :, 1, :]
                    src = bank(2 + L % 2).rearrange("p (b h) -> p b h", h=h)
                    m = mk[:, (L - 1) * HALF:L * HALF].rearrange("p (b h) -> p b h", h=h)
                    dve.copy_predicated(dst, m, src).then_inc(scores_kept, 1)

                dve.wait_ge(fq_loaded, 32 * j + 32)
                dve.wait_ge(k_turned, j + 1)
                dve.tensor_scalar(hK[:, :], fF[:, :], -1.0, 1.0, ALU.mult, ALU.add).then_inc(scaled, 1)
                dve.wait_ge(read_done, j + 1)
                link(dve.tensor_tensor(hQ[:, :], fQ[:, :], fF[:, :], ALU.mult))
                dve.wait_ge(scaled, 9 * j + 1)
                dve.nop().then_inc(scaled, 1)
                keep_scores(0)
                before, size = fF[:, :], T
                used = 0
                for L in range(2, LEVELS + 1):
                    s = 1 << (L - 2)
                    tt = before.rearrange("p (b two) -> p b two", two=2)
                    kk = hK[:, :].rearrange("p (b two s) -> p b two s", two=2, s=s)
                    qq = hQ[:, :].rearrange("p (b two s) -> p b two s", two=2, s=s)
                    nb = T // (2 * s)
                    after = tot[:, used:used + nb]
                    used += nb
                    dve.wait_ge(scores_done, 8 * j + L)
                    link(dve.tensor_tensor(kk[:, :, 0, :], kk[:, :, 0, :],
                                           tt[:, :, 1:2].to_broadcast([P, nb, s]), ALU.mult))
                    link(dve.tensor_tensor(qq[:, :, 1, :], qq[:, :, 1, :],
                                           tt[:, :, 0:1].to_broadcast([P, nb, s]), ALU.mult))
                    link(dve.tensor_tensor(after, tt[:, :, 0], tt[:, :, 1], ALU.mult))
                    dve.nop().then_inc(scaled, 1)
                    keep_scores(L - 1)
                    before = after
                dve.wait_ge(outer_done, j + 1)
                for c in range(TT - 1):
                    kv = ps[:, 2 * HALF + c * P:2 * HALF + (c + 1) * P]
                    if c == 0:
                        dve.tensor_copy(st[:, 1, :], kv).then_inc(state_step, 1)
                    else:
                        dve.wait_ge(state_step, 7 * j + c)
                        dve.scalar_tensor_tensor(st[:, c + 1, :], st[:, c, :], before[:, c:c + 1], kv,
                                                 ALU.mult, ALU.add).then_inc(state_step, 1)
                for q in range(4):
                    split(P_MIX + 16 + q, 4 * j)
                dve.wait_ge(read_sq, j + 1)
                dve.tensor_reduce(sso[:, :], junk[:, :].rearrange("p (c v) -> p c v", c=TT), AX_X,
                                  ALU.add).then_inc(read_ss, 1)
                dve.wait_ge(read_rstd, j + 1)
                dve.wait_ge(gate_gained, j + 1)
                for c in range(TT):
                    last = dve.scalar_tensor_tensor(hG[:, c, :], ps[:, c * P:(c + 1) * P], rso[:, c:c + 1],
                                                    hG[:, c, :], ALU.mult, ALU.mult)
                last.then_inc(ro_ready, 1)

            per_head = 1 + 3 * 7
            dve.wait_ge(ext_stored, 16)
            dve.nop().then_inc(read_ss, 1)
            dve.nop().then_inc(ro_ready, 1)
            with dve.Fori(0, HH) as j:
                head(j)

            dve.nop().then_inc(qk_ss, 1)

            def sum_qk(pp, w, i):
                dve.wait_ge(qk_sq, 2 * pp + w + 1 + 4 * i)
                dve.tensor_reduce(ssq[:, w, :], junk[:, :].rearrange("p (g d) -> p g d", d=DH), AX_X,
                                  ALU.add).then_inc(qk_ss, 1)

            def norm_qk(pp, w, i):
                dve.wait_ge(qk_rstd, 2 * pp + w + 1 + 4 * i)
                v = (qin, kin)[w].rearrange("p t (h d) -> p (t h) d", d=DH)
                r = rsq[:, w, :].unsqueeze(2).to_broadcast([P, 16, DH])
                dve.tensor_tensor(v, v, r, ALU.mult).then_inc(qk_normed, 1)

            def two_pairs(i):
                def head_output(pp, hd):
                    dve.wait_ge(unit_out, NU * pp + NU - 1 + hd + 2 * NU * i)
                    dve.reciprocal(rcp[:, hd, :], psumr[:, pp, hd, :]).then_inc(rcp_ready, 1)
                    dve.wait_ge(rcp_ready, 2 * pp + hd + 1 + 4 * i)
                    dve.tensor_tensor(cat[:, :, ds((4 * i + 2 * pp + hd) * DH, DH)],
                                      bank(6 + hd).rearrange("p (t d) -> p t d", d=DH),
                                      rcp[:, hd, :].unsqueeze(2).to_broadcast([P, TT, DH]), ALU.mult)\
                       .then_inc(head_out, 1)

                sum_qk(0, 0, i)
                sum_qk(0, 1, i)
                norm_qk(0, 0, i)
                norm_qk(0, 1, i)
                for v in range(2 * NU + 1):
                    if v < 2 * NU:
                        pp, hd, parts = unit(v)
                        dve.wait_ge(unit_scores, v + 1 + 2 * NU * i)
                        if v in (0, NU):
                            dve.wait_ge(bias_masked, 4 * pp + 4 + 8 * i)
                        if v >= 2:
                            dve.wait_ge(unit_exp, v - 1 + 2 * NU * i)
                        dve.nop().then_inc(dve_passed, 1)
                        for t, n, c0 in parts:
                            b = 2 * (v % 2) * HALF
                            last = dve.tensor_tensor_reduce(
                                S[:, v % 2, c0:c0 + n * P], ps[:, b + c0:b + c0 + n * P],
                                bias[:, pp, hd, BAND - n * P:BAND], -1.0, 3.0e38, ALU.add, ALU.min,
                                nmax[:, hd, t:t + 1])
                        last.then_inc(unit_max, 1)
                    if v >= 1 and not by_scalar(v - 1):
                        dve.wait_ge(unit_turned, v + 2 * NU * i)
                        if v >= 3:
                            dve.wait_ge(unit_out, v - 2 + 2 * NU * i)
                        dve.tensor_copy(PT[:, (v - 1) % 2, :], ps[:, 4 * HALF:4 * HALF + BAND])\
                           .then_inc(PT_by_vector, 1)
                    if v in SUM_AT:
                        sum_qk(1, SUM_AT.index(v), i)
                    if v in NORM_AT:
                        norm_qk(1, NORM_AT.index(v), i)
                    if v in (NU, NU + 1):
                        head_output(0, v - NU)
                head_output(1, 0)
                head_output(1, 1)

            dve.wait_ge(ro_stored, 16 * HH)
            with dve.Fori(0, 2) as i:
                two_pairs(i)

            hT_lo(R_CAT, 0)
            hT_lo(R_CAT, 1)
            for t in range(TT):
                if t == TT - 1:
                    for q in range(4):
                        split(P_OUT + 4 + q)
                add(A_OUT + t, 0, t, 0, 1.0)
                if t + 2 < TT:
                    hT_lo(R_CAT, t + 2)
            for t in range(TT):
                if t == TT - 1:
                    split(P_FFN2)
                    split(P_FFN2 + 1)
                add(A_OUT + 8 + t, 0, t, 1, 1.0)
                if t >= 1:
                    hT_lo(R_FFN2, t - 1)
                normalise(R_FFN2, t)
            hT_lo(R_FFN2, TT - 1)
            ffn(1, P_FFN2, A_FFN2, False)

        @block.gpsimd
        def _(pool):
            pool.memset(mhalf[:, :], -0.5).then_inc(mhalf_set, 1)
            pool.dma_start(gain[:, :], ffn1_norm_g[0:1, :].to_broadcast([P, D])).then_inc(gain_loaded, 16)
            pool.dma_start(lbs[:, :, :], hgrn_lower_bounds.rearrange("r (h p) -> p r h", p=P),
                           allow_slow_non_contiguous=True).then_inc(lb_loaded, 16)
            pool.dma_start(gn[:, :], hgrn_out_norm_g[0:1, :].to_broadcast([P, P])).then_inc(gn_loaded, 16)
            pool.dma_start(qkg[0:DH, 0:1], attn_q_norm_g.rearrange("a d -> d a"),
                           allow_slow_non_contiguous=True).then_inc(qk_gain_loaded, 16)
            pool.dma_start(qkg[DH:P, 0:1], attn_q_norm_g.rearrange("a d -> d a"),
                           allow_slow_non_contiguous=True).then_inc(qk_gain_loaded, 16)
            pool.dma_start(qkg[0:DH, 1:2], attn_k_norm_g.rearrange("a d -> d a"),
                           allow_slow_non_contiguous=True).then_inc(qk_gain_loaded, 16)
            pool.dma_start(qkg[DH:P, 1:2], attn_k_norm_g.rearrange("a d -> d a"),
                           allow_slow_non_contiguous=True).then_inc(qk_gain_loaded, 16)
            pool.wait_ge(mhalf_set, 1)

            def rms(R):
                for t in range(TT):
                    q = TT * norm_no(R) + t
                    pool.wait_ge(ss_ready, q + 1)
                    pool.tensor_scalar(rstd[:, q:q + 1], ss[:, q:q + 1], 1.0 / D, EPS, ALU.mult, ALU.add)\
                        .then_inc(var_ready, 1)
                    pool.wait_ge(var_ready, q + 1)
                    pool.tensor_tensor(rstd[:, q:q + 1], rstd[:, q:q + 1], mhalf[:, 0:1], ALU.pow)\
                        .then_inc(rstd_ready, 1)

            rms(R_FFN1)
            pool.wait_ge(y_ready, TT)
            pool.dma_start(gain[:, :], mix_norm_g[0:1, :].to_broadcast([P, D])).then_inc(gain_loaded, 16)
            rms(R_MIX)

            def stored(n):
                for s in range(2):
                    pool.wait_ge(proj_stored[s], 64 * n)

            def load_fq(j):
                pool.dma_start(fF[:, :], feat[ds(j * P + HALF, P), :]).then_inc(fq_loaded, 16)
                pool.dma_start(fQ[:, :], feat[ds(j * P, P), :]).then_inc(fq_loaded, 16)

            def load_v(j):
                pool.dma_start(hV[:, :, :], tok[:, 0, ds(j * P, P)].rearrange("(t p) c -> p t c", p=P))\
                    .then_inc(v_loaded, 16)

            def load_g(j):
                pool.dma_start(hG[:, :, :], tok[:, 1, ds(j * P, P)].rearrange("(t p) c -> p t c", p=P))\
                    .then_inc(g_loaded, 16)

            def finish(j):
                pool.wait_ge(gn_loaded, 16)
                pool.wait_ge(g_loaded, 16 * j + 16)
                gb = bass.AP(gn, 0, [list(gn[:, :].ap[0]), [0, TT], [1, P]])
                pool.tensor_tensor(hG[:, :, :], hG[:, :, :], gb, ALU.mult).then_inc(gate_gained, 1)
                pool.wait_ge(read_ss, j + 2)
                pool.nop().then_inc(pool_passed, 1)
                pool.tensor_scalar(rso[:, :], sso[:, :], 1.0 / P, EPS, ALU.mult, ALU.add).then_inc(read_var, 1)
                pool.wait_ge(read_var, j + 1)
                pool.tensor_tensor(rso[:, :], rso[:, :], mhalf[:, 0:TT], ALU.pow).then_inc(read_rstd, 1)
                pool.wait_ge(ro_ready, j + 2)
                pool.dma_start(ro_d[:, ds(j * P, P)].rearrange("(t p) c -> p t c", p=P), hG[:, :, :])\
                    .then_inc(ro_stored, 16)

            pool.wait_ge(x_added, A_OUT)
            pool.dma_start(tot[:, 0:(LEVELS - 1) * 64], masks).then_inc(mask_loaded, 16)
            pool.dma_start(relrow, attn_rel_bias[0]).then_inc(rel_loaded, 16)
            pool.wait_ge(ext_step, 3)
            pool.dma_start(ext_d, extrow).then_inc(ext_stored, 16)
            pool.wait_ge(ext_stored, 16)
            skew = bass.AP(ext_d.tensor, P - 1, [[EXT, AH], [-1, P], [1, BAND]])
            pool.dma_start(bias_d, skew).then_inc(bias_stored, 16)
            stored(2)
            load_fq(0)
            stored(3)
            load_v(0)
            stored(4)
            load_g(0)
            with pool.Fori(0, HH - 1) as j:
                pool.wait_ge(scores_done, 8 * j + 1)
                pool.wait_ge(scaled, 9 * j + 3)
                load_fq(j + 1)
                finish(j)
                pool.wait_ge(read_done, j + 2)
                load_v(j + 1)
                pool.wait_ge(ro_stored, 16 * j + 16)
                load_g(j + 1)
            finish(HH - 1)

            def load_qk(p):
                for w in range(2):
                    pool.dma_start((qin, kin)[w], tok[:, 2 + w, ds(p * P, P)].rearrange("(t p) c -> p t c", p=P))\
                        .then_inc(qk_loaded[w], 16)

            def load_v_bias(i, pp):
                p = 2 * i + pp
                pool.dma_start(vin[:, pp, :, :], tok[:, 4, ds(p * P, P)].rearrange("(t p) c -> p t c", p=P))\
                    .then_inc(av_loaded[pp], 16)
                pool.dma_start(bias[:, pp, :, :], bias_d[ds(2 * p, 2), :, :].rearrange("h t s -> t h s"))\
                    .then_inc(bias_loaded, 16)
                pool.wait_ge(bias_loaded, 32 * i + 16 * pp + 16)
                for hd in range(2):
                    pool.memset(bias[CHUNK:P, pp, hd, 0:CHUNK], MASKED).then_inc(bias_masked, 1)
                    pool.memset(bias[0:CHUNK, pp, hd, BAND - CHUNK:BAND], MASKED).then_inc(bias_masked, 1)

            def qk_rms(i, pp):
                for w in range(2):
                    n = 4 * i + 2 * pp + w
                    pool.wait_ge(qk_ss, n + 2)
                    pool.tensor_scalar(rsq[:, w, :], ssq[:, w, :], 1.0 / DH, EPS, ALU.mult, ALU.add)\
                        .then_inc(qk_var, 1)
                    pool.wait_ge(qk_var, n + 1)
                    pool.tensor_tensor(rsq[:, w, :], rsq[:, w, :], mhalf[:, 0:16], ALU.pow).then_inc(qk_rstd, 1)

            pool.wait_ge(bias_stored, 16)
            stored(6)
            pool.wait_ge(y_ready, 2 * TT)
            pool.wait_ge(turned, 2 * TT)
            load_qk(0)
            pool.wait_ge(proj_done, 56)
            stored(7)
            load_v_bias(0, 0)
            pool.wait_ge(bias_masked, 4)
            qk_rms(0, 0)
            pool.wait_ge(qk_turned, 2)
            load_qk(1)
            load_v_bias(0, 1)
            pool.wait_ge(ro_stored, 16 * HH)
            pool.dma_start(cat[:, :, HALF:D], ro_d.rearrange("(t p) c -> p t c", p=P)).then_inc(cat_loaded, 16)
            pool.wait_ge(bias_masked, 8)
            qk_rms(0, 1)
            pool.wait_ge(qk_turned, 4)
            load_qk(2)
            pool.wait_ge(unit_out, NU)
            load_v_bias(1, 0)
            pool.wait_ge(bias_masked, 12)
            qk_rms(1, 0)
            pool.wait_ge(qk_turned, 6)
            load_qk(3)
            pool.wait_ge(unit_out, 2 * NU)
            load_v_bias(1, 1)
            pool.wait_ge(bias_masked, 16)
            qk_rms(1, 1)
            pool.wait_ge(qk_turned, 8)
            pool.dma_start(gain[:, :], ffn2_norm_g[0:1, :].to_broadcast([P, D])).then_inc(gain_loaded, 16)
            rms(R_FFN2)


_NAMES = ["x", "ffn1_norm_g", "ffn1_w_gate", "ffn1_w_up", "ffn1_w_down", "mix_norm_g", "w_in",
          "attn_q_norm_g", "attn_k_norm_g", "attn_rel_bias", "hgrn_lower_bounds", "hgrn_out_norm_g",
          "w_out", "ffn2_norm_g", "ffn2_w_gate", "ffn2_w_up", "ffn2_w_down"]


def kernel(**inputs):
    import concourse.bacc as bacc
    from concourse.bass_utils import run_bass_kernel_spmd

    nc = bacc.Bacc("TRN2", target_bir_lowering=False, num_devices=1)
    arrays = {n: np.ascontiguousarray(inputs[n]) for n in _NAMES}
    arrays["identity"] = np.eye(P, dtype=np.float32)
    arrays["masks"] = level_masks()
    args = [nc.dram_tensor(n, a.shape, mybir.dt.from_np(a.dtype), kind="ExternalInput").ap()
            for n, a in arrays.items()]
    out = nc.dram_tensor("out", (1, T, D), F32, kind="ExternalOutput").ap()
    build(nc, *args, out)
    r = run_bass_kernel_spmd(nc, [arrays], core_ids=[0])
    return r.results[0]["out"]
```

```python
from contextlib import ExitStack

import numpy as np

import concourse.bass as bass
from concourse import mybir

F32 = mybir.dt.float32
F32R = mybir.dt.float32r
U8 = mybir.dt.uint8
ALU = mybir.AluOpType
ACT = mybir.ActivationFunctionType
AX_X = mybir.AxisListType.X

P = 128
T = 1024
D = 1024
TT = T // P
KT = D // P
HALF = 512
D_FF = 2816
FT = D_FF // P
NG = FT // 2
AH = 8
DH = 64
PROJ_OUTS = 8 * 7
HH = 4
CHUNK = 64
KEY_TILES = 5
BAND = KEY_TILES * P
N_REL = 257
REL_CLIP = 128
EXT = 768
EPS = 1e-6
MASKED = -1.0e30

RING = 4
PIECES_FFN = 3 * FT
PIECES_MIX = 4 * 7
PIECES_OUT = 8
P_FFN1 = 0
P_MIX = P_FFN1 + PIECES_FFN
P_OUT = P_MIX + PIECES_MIX
P_FFN2 = P_OUT + PIECES_OUT

ADDS_FFN = NG * 16
A_FFN1 = 0
A_OUT = A_FFN1 + ADDS_FFN
A_FFN2 = A_OUT + 16

R_FFN1, R_MIX, R_CAT, R_FFN2 = range(4)

LEVEL_AT = {2: 0, 3: 1, 5: 2, 6: 3, 8: 4, 9: 5, 10: 6, 12: 7}
TURN_AT, OUTER_AT, READ_AT = 13, 14, 15
LEVELS = 8

FEATURE_ORDER = [(0, 0), (1, 0), (0, 1), (1, 1), (2, 0), (3, 0), (2, 1), (3, 1)]

UNITS = [[(7, 5, 0)], [(6, 5, 0)], [(5, 5, 0)], [(4, 5, 0)],
         [(3, 4, 0), (0, 1, 4 * P)], [(2, 3, 0), (1, 2, 3 * P)]]
NU = 2 * len(UNITS)
PAIRS = AH // 2
NV = NU * PAIRS
SQUARE_AT, SUM_AT, NORM_AT, TURN_QK_AT = (2, 5), (4, 7), (6, 9), (8, 10)
TURN_OUT_AT = (NU - 1, NU + 2)


CAT_ORDER = (4, 5, 6, 7, 0, 1, 2, 3)


def out_bank(p, g):
    return 5 if (p, g) == (PAIRS - 1, 1) else 4


def unit(v):
    return v // NU, v % 2, UNITS[(v % NU) // 2]


def by_scalar(v):
    return v % 3 == 2


def extra(v):
    found = [("qk", v // NU + 1, w) for w in range(2)
             if v < NV - NU and v % NU == TURN_QK_AT[w]]
    found += [("out", p, g) for p in range(PAIRS) for g in range(2) if v == NU * p + TURN_OUT_AT[g]]
    return found[0] if found else None


def turn_bank(R, t):
    if R == R_FFN1:
        return 2 * t if t < 4 else 4 + 2 * (t % 2)
    if R == R_FFN2:
        return 4 if t == 7 else 2 * ((t + 1) % 2)
    return 2 * (t % 2)


def level_masks():
    m = np.zeros((P, LEVELS - 1, P // 2), np.float32)
    for level in range(1, LEVELS):
        h = 1 << (level - 1)
        for b in range(P // (2 * h)):
            m[2 * h * b:2 * h * b + h, level - 1, b * h:(b + 1) * h] = 1
    return m.reshape(P, -1)


def build(nc, x, ffn1_norm_g, ffn1_w_gate, ffn1_w_up, ffn1_w_down, mix_norm_g, w_in, attn_q_norm_g,
          attn_k_norm_g, attn_rel_bias, hgrn_lower_bounds, hgrn_out_norm_g, w_out, ffn2_norm_g,
          ffn2_w_gate, ffn2_w_up, ffn2_w_down, identity, masks, out):
    ds = bass.DynSlice
    with ExitStack() as ctx:
        feat = nc.dram_tensor("feat_scratch", [2 * HH * P, T], F32, kind="Internal").ap()
        tok = nc.dram_tensor("tok_scratch", [T, 5, HALF], F32, kind="Internal").ap()
        ro_d = nc.dram_tensor("ro_scratch", [T, HALF], F32, kind="Internal").ap()
        bias_d = nc.dram_tensor("bias_scratch", [AH, P, BAND], F32, kind="Internal").ap()
        ext_d = nc.dram_tensor("ext_scratch", [AH, EXT], F32, kind="Internal").ap()

        def keep(name, shape, dt=F32, where=ctx, side="left"):
            return where.enter_context(nc.sbuf_tensor(name, shape, dt, side=side))

        def sem(name):
            return ctx.enter_context(nc.semaphore(name))

        xs = keep("xs", [P, TT, D])
        raw = keep("raw", [P, RING, 1024])
        whi = keep("whi", [P, RING, 1024], F32R)
        wlo = keep("wlo", [P, RING, 1024], F32R)
        y = keep("y", [P, 2, D])
        junk = keep("junk", [P, 1024])
        gain = keep("gain", [P, D])
        ident = keep("ident", [P, P])
        ss = keep("ss", [P, 3 * TT])
        rstd = keep("rstd", [P, 3 * TT])
        mhalf = keep("mhalf", [P, 16])
        lbs = keep("lbs", [P, 2, HH])
        lb = keep("lb", [P, 3, HH])
        gn = keep("gn", [P, P])
        qkg = keep("qkg", [P, 2])
        ssq = keep("ssq", [P, 2, 16])
        rsq = keep("rsq", [P, 2, 16])

        with ExitStack() as c:
            hThi = keep("hThi", [P, KT, T], F32R, c)
            hTlo = keep("hTlo", [P, KT, T], F32R, c)
        with ExitStack() as c:
            vin = keep("v_in", [P, 2, TT, P], where=c)
            qT = keep("qT", [P, 2, T], where=c)
            kT = keep("kT", [P, 2, T], where=c)
            bias = keep("bias", [P, 2, 2, BAND], where=c)
            S = keep("S", [P, 2, BAND], where=c)
            Pr = keep("Pr", [P, 2, BAND], where=c)
            PT = keep("PT", [P, 2, BAND], where=c)
            nmax = keep("nmax", [P, 2, TT], where=c)
            used = 4 * (4 * T + 2 * TT * P + 4 * BAND + 6 * BAND + 2 * TT)
            keep("clear_of_hT", [P, (4 * 2 * KT * T - used) // 4], where=c)
            psumr = keep("psumr", [P, 2, 2, TT], where=c)
            rcp = keep("rcp", [P, 2, 2, TT], where=c)
            outT = keep("outT", [P, 2, T], where=c)
        with ExitStack() as c:
            hidhi = keep("hidhi", [P, 2, 2, T], F32R, c, "right")
            hidlo = keep("hidlo", [P, 2, 2, T], F32R, c, "right")
            sil = keep("sil", [P, 2, HALF], where=c, side="right")
            prod = keep("prod", [P, 2, HALF], where=c, side="right")
        with ExitStack() as c:
            fF = keep("fF", [P, T], where=c, side="right")
            fQ = keep("fQ", [P, T], where=c, side="right")
            hK = keep("hK", [P, T], where=c, side="right")
            hQ = keep("hQ", [P, T], where=c, side="right")
            hV = keep("hV", [P, TT, P], where=c, side="right")
            hG = keep("hG", [P, TT, P], where=c, side="right")
            tot = keep("tot", [P, T], where=c, side="right")
            aT = keep("aT", [P, T], where=c, side="right")
            kS = keep("kS", [P, TT, P], where=c, side="right")
            st = keep("st", [P, TT, P], where=c, side="right")
            mk = keep("mk", [P, (LEVELS - 1) * HALF], U8, c, "right")
            sso = keep("sso", [P, TT], where=c, side="right")
            rso = keep("rso", [P, TT], where=c, side="right")
        with ExitStack() as c:
            cat = keep("cat", [P, TT, D], where=c, side="right")

        qin = y[:, 1, :].rearrange("p (t c) -> p t c", t=TT)
        kin = gain[:, :].rearrange("p (t c) -> p t c", t=TT)
        relrow = aT[0:AH, 0:N_REL]
        extrow = kS[0:AH, :, :].rearrange("p a b -> p (a b)")[:, 0:EXT]

        def y_slot(R, t):
            if R == R_FFN1 and t >= 2:
                return (fF[:, :], fQ[:, :], hK[:, :], hQ[:, :], hV[:, :, :].rearrange("p a b -> p (a b)"),
                        hG[:, :, :].rearrange("p a b -> p (a b)"))[t - 2]
            return y[:, t % 2, :]

        ps = ctx.enter_context(nc.psum_tensor("ps", [P, 8 * HALF], F32))

        def bank(b, n=HALF):
            return ps[:, b * HALF:b * HALF + n]

        x_loaded = [sem(f"x_loaded{t}") for t in range(TT)]
        ident_loaded = sem("ident_loaded")
        lb_loaded = sem("lb_loaded")
        gn_loaded = sem("gn_loaded")
        gain_loaded = sem("gain_loaded")
        mhalf_set = sem("mhalf_set")
        raw_loaded = [sem(f"raw_loaded{s}") for s in range(RING)]
        split_hi = sem("split_hi")
        split_lo = sem("split_lo")
        piece_used = sem("piece_used")
        ss_ready = sem("ss_ready")
        var_ready = sem("var_ready")
        rstd_ready = sem("rstd_ready")
        y_ready = sem("y_ready")
        turned = sem("turned")
        hT_hi_ready = sem("hT_hi_ready")
        hT_ready = sem("hT_ready")
        gate_done = sem("gate_done")
        up_done = sem("up_done")
        silu_done = sem("silu_done")
        prod_done = sem("prod_done")
        hid_hi_ready = sem("hid_hi_ready")
        hid_ready = sem("hid_ready")
        row_done = sem("row_done")
        x_added = sem("x_added")
        out_stored = sem("out_stored")
        proj_done = sem("proj_done")
        proj_evac = sem("proj_evac")
        proj_stored = [sem(f"proj_stored{s}") for s in range(2)]
        lb_diff = sem("lb_diff")
        lb_sig = sem("lb_sig")
        lb_ready = sem("lb_ready")
        sig_ready = sem("sig_ready")
        mask_loaded = sem("mask_loaded")
        mask_set = sem("mask_set")
        fq_loaded = sem("fq_loaded")
        v_loaded = sem("v_loaded")
        g_loaded = sem("g_loaded")
        hgrn_step = sem("hgrn_step")
        scaled = sem("scaled")
        scores_done = sem("scores_done")
        scores_kept = sem("scores_kept")
        k_turned = sem("k_turned")
        k_rows = sem("k_rows")
        outer_done = sem("outer_done")
        state_step = sem("state_step")
        read_done = sem("read_done")
        read_sq = sem("read_sq")
        read_ss = sem("read_ss")
        read_var = sem("read_var")
        read_rstd = sem("read_rstd")
        gate_gained = sem("gate_gained")
        ro_gated = sem("ro_gated")
        ro_ready = sem("ro_ready")
        ro_stored = sem("ro_stored")
        rel_loaded = sem("rel_loaded")
        ext_step = sem("ext_step")
        ext_stored = sem("ext_stored")
        bias_stored = sem("bias_stored")
        qk_gain_loaded = sem("qk_gain_loaded")
        qk_gain_ready = sem("qk_gain_ready")
        qk_loaded = [sem(f"{w}_loaded") for w in "qk"]
        av_loaded = [sem(f"av_loaded{p}") for p in range(2)]
        bias_loaded = sem("bias_loaded")
        bias_masked = sem("bias_masked")
        qk_sq = sem("qk_sq")
        qk_ss = sem("qk_ss")
        qk_var = sem("qk_var")
        qk_rstd = sem("qk_rstd")
        qk_normed = sem("qk_normed")
        qk_turned = sem("qk_turned")
        qkT_ready = sem("qkT_ready")
        unit_scores = sem("unit_scores")
        unit_max = sem("unit_max")
        unit_exp = sem("unit_exp")
        unit_turned = sem("unit_turned")
        PT_by_vector = sem("PT_by_vector")
        PT_by_scalar = sem("PT_by_scalar")
        unit_out = sem("unit_out")
        outT_ready = sem("outT_ready")
        out_turned = sem("out_turned")
        rcp_ready = sem("rcp_ready")
        head_out = sem("head_out")
        cat_loaded = sem("cat_loaded")
        pool_passed = sem("pool_passed")

        block = ctx.enter_context(nc.Block())

        def wait_PT(eng, v):
            if by_scalar(v):
                eng.wait_ge(PT_by_scalar, (v + 1) // 3)
            else:
                eng.wait_ge(PT_by_vector, v + 1 - (v + 1) // 3)

        def score_bank(v):
            return 2 * ((v + 1) % 2)

        def norm_no(R):
            return R if R < R_CAT else 2

        @block.sync
        def _(sp):
            def piece(n0, adv, src, shape):
                if n0 >= RING:
                    sp.wait_ge(split_lo, n0 - RING + 1 + adv)
                dst = raw[:, n0 % RING, :]
                if shape:
                    dst = dst.rearrange("p (k c) -> p k c", k=shape)
                sp.dma_start(dst, src).then_inc(raw_loaded[n0 % RING], 16)

            def ffn(base, w_gate, w_up, w_down):
                wg = w_gate[0].rearrange("(k p) f -> p k f", p=P)
                wu = w_up[0].rearrange("(k p) f -> p k f", p=P)

                def gate_up(f, n0, adv):
                    piece(n0, adv, wg[:, :, ds(f * P, P)], KT)
                    piece(n0 + 1, adv, wu[:, :, ds(f * P, P)], KT)

                def down(f, n0, adv):
                    piece(n0, adv, w_down[0][ds(f * P, P), :], 0)

                gate_up(0, base, 0)
                if base == P_FFN1:
                    for t in range(4, TT):
                        sp.dma_start(xs[:, t, :], x[0, t * P:(t + 1) * P, :]).then_inc(x_loaded[t], 16)
                gate_up(1, base + 2, 0)
                with sp.Fori(0, NG // 2) as i:
                    for g in range(2):
                        n0 = base + 4 + 6 * g
                        gate_up(4 * i + 2 + 2 * g, n0, 12 * i)
                        gate_up(4 * i + 3 + 2 * g, n0 + 2, 12 * i)
                        down(4 * i + 2 * g, n0 + 4, 12 * i)
                        down(4 * i + 2 * g + 1, n0 + 5, 12 * i)
                down(FT - 2, base + PIECES_FFN - 2, 0)
                down(FT - 1, base + PIECES_FFN - 1, 0)

            for t in range(4):
                sp.dma_start(xs[:, t, :], x[0, t * P:(t + 1) * P, :]).then_inc(x_loaded[t], 16)
            ffn(P_FFN1, ffn1_w_gate, ffn1_w_up, ffn1_w_down)

            wi = w_in[0].rearrange("(q k p) c -> q p k c", p=P, k=2)

            def mix_group(col, n0, adv):
                for q in range(4):
                    piece(n0 + q, adv, wi[q][:, :, ds(col, HALF)], 2)

            with sp.Fori(0, 4) as n:
                mix_group(HALF * n + 3 * HALF, P_MIX, 4 * n)
            with sp.Fori(0, 3) as n:
                mix_group(HALF * n, P_MIX + 16, 4 * n)
            wo = w_out[0].rearrange("(q k p) c -> q p k c", p=P, k=2)
            for h in range(2):
                for q in range(4):
                    piece(P_OUT + 4 * h + q, 0, wo[q][:, :, h * HALF:(h + 1) * HALF], 2)
            ffn(P_FFN2, ffn2_w_gate, ffn2_w_up, ffn2_w_down)

        @block.tensor
        def _(pe):
            def three(dst, a, b, first, last):
                (ahi, alo), (bhi, blo) = a, b
                pe.matmul(dst, ahi, bhi, start=first, stop=False)
                pe.matmul(dst, ahi, blo, start=False, stop=False)
                return pe.matmul(dst, alo, bhi, start=False, stop=last)

            def turn_tile(R, t):
                r = TT * R + t
                if R == R_CAT:
                    if t == 0:
                        pe.wait_ge(head_out, 2 * PAIRS - 1)
                        pe.wait_ge(cat_loaded, 16)
                        pe.wait_ge(unit_max, NV)
                    src = cat[:, CAT_ORDER[t], :]
                else:
                    q = TT * norm_no(R) + t
                    pe.wait_ge(y_ready, q + 1)
                    src = y_slot(R, t)
                if r >= 4:
                    pe.wait_ge(hT_ready, r - 1)
                if t < 2 and R == R_MIX:
                    pe.wait_ge(prod_done, 2 * FT)
                c0 = turn_bank(R, t) * HALF
                for k in range(KT):
                    mm = pe.transpose(ps[:, c0 + k * P:c0 + (k + 1) * P],
                                      src[:, k * P:(k + 1) * P], ident[:, :])
                mm.then_inc(turned, 1)

            def ffn(F, base, adds, R):
                e_base = 2 * FT * F

                def product(which, h, f0, advf, n0, adv, turns=()):
                    s = (n0 + which) % RING
                    e = e_base + 2 * f0 + h
                    pe.wait_ge(split_lo, n0 + which + 1 + adv)
                    if f0 and which == 0:
                        pe.wait_ge(silu_done, e - 1 + 2 * advf)
                    elif f0:
                        pe.wait_ge(prod_done, e - 1 + 2 * advf)
                    for k in range(KT):
                        mm = three(bank(2 * which + h),
                                   [w[:, s, k * P:(k + 1) * P] for w in (whi, wlo)],
                                   [a[:, k, h * HALF:(h + 1) * HALF] for a in (hThi, hTlo)],
                                   k == 0, k == KT - 1)
                        if k == KT // 2 - 1:
                            for t in turns:
                                turn_tile(R, t)
                    mm.then_inc((gate_done, up_done)[which], 1)

                def gate_up(f0, advf, n0, adv):
                    for which in range(2):
                        for h in range(2):
                            product(which, h, f0, advf, n0, adv)

                def first_tile():
                    r = TT * R
                    if R == R_FFN1:
                        pe.wait_ge(hT_ready, r + 4)
                        product(0, 0, 0, 0, base, 0, turns=(4,))
                        turn_tile(R, 5)
                        product(1, 0, 0, 0, base, 0, turns=(6, 7))
                    else:
                        pe.wait_ge(hT_ready, r + 6)
                        product(0, 0, 0, 0, base, 0)
                        turn_tile(R, 7)
                        pe.wait_ge(hT_ready, r + 7)
                        product(1, 0, 0, 0, base, 0)
                    pe.wait_ge(hT_ready, r + 8)
                    product(0, 1, 0, 0, base, 0)
                    product(1, 1, 0, 0, base, 0)

                def down(g0, advg, n0, adv, tail=None):
                    par = g0 % 2
                    pe.wait_ge(split_lo, n0 + 2 + adv)
                    pe.wait_ge(hid_ready, e_base + 4 * g0 + 4 + 4 * advg)
                    for t in range(TT):
                        for h in range(2):
                            d = adds + 16 * g0 + 2 * t + h
                            if d >= 4:
                                pe.wait_ge(x_added, d - 3 + 16 * advg)
                            for j in range(2):
                                s = (n0 + j) % RING
                                mm = three(bank(4 + d % 4),
                                           [a[:, par, j, t * P:(t + 1) * P] for a in (hidhi, hidlo)],
                                           [w[:, s, h * HALF:(h + 1) * HALF] for w in (whi, wlo)],
                                           j == 0, j == 1)
                            mm.then_inc(row_done, 1)
                        if tail is not None and t >= 2:
                            turn_tile(tail, t - 2)

                first_tile()
                gate_up(1, 0, base + 2, 0)
                with pe.Fori(0, NG // 2) as i:
                    for g in range(2):
                        n0 = base + 4 + 6 * g
                        gate_up(2 + 2 * g, 4 * i, n0, 12 * i)
                        gate_up(3 + 2 * g, 4 * i, n0 + 2, 12 * i)
                        down(g, 2 * i, n0 + 4, 12 * i)
                down(NG - 1, 0, base + PIECES_FFN - 2, 0, tail=R_MIX if F == 0 else None)

            pe.wait_ge(ident_loaded, 16)
            for t in range(4):
                turn_tile(R_FFN1, t)
            ffn(0, P_FFN1, A_FFN1, R_FFN1)

            def group(n0, advn, feature, hook):
                base = P_MIX + 4 * n0
                for o in range(8):
                    idx = 8 * n0 + o
                    if idx >= 4:
                        pe.wait_ge(proj_evac, idx - 3 + 8 * advn)
                    else:
                        pe.wait_ge(x_added, A_OUT)
                    if n0 == 0:
                        pe.wait_ge(hT_ready, TT * R_MIX + (4 if o < 2 else 8))
                    for k in range(KT):
                        s = (base + k // 2) % RING
                        if o == 0 and k % 2 == 0:
                            pe.wait_ge(split_lo, base + k // 2 + 1 + 4 * advn)
                        c0 = (k % 2) * HALF
                        if feature:
                            f, h = FEATURE_ORDER[o]
                            a = [w[:, s, c0 + f * P:c0 + (f + 1) * P] for w in (whi, wlo)]
                            b = [v[:, k, h * HALF:(h + 1) * HALF] for v in (hThi, hTlo)]
                        else:
                            a = [v[:, k, o * P:(o + 1) * P] for v in (hThi, hTlo)]
                            b = [w[:, s, c0:c0 + HALF] for w in (whi, wlo)]
                        mm = three(bank(4 + o % 4), a, b, k == 0, k == KT - 1)
                        if o == 7 and k % 2 == 1 and k < KT - 1:
                            mm.then_inc(piece_used, 1)
                        if k == 3:
                            hook(2 * o)
                    mm.then_inc(proj_done, 1)
                    hook(2 * o + 1)

            def hgrn(j):
                def hook(at):
                    if at in LEVEL_AT:
                        L = LEVEL_AT[at]
                        pe.wait_ge(scaled, 9 * j + L + 1)
                        if L == 0:
                            pe.wait_ge(ro_ready, j + 1)
                            for c in range(TT):
                                mm = pe.matmul(ps[:, c * P:(c + 1) * P], hK[:, c * P:(c + 1) * P],
                                               fQ[:, c * P:(c + 1) * P], start=True, stop=True)
                        else:
                            h = 1 << (L - 1)
                            if L >= 3:
                                pe.wait_ge(scores_kept, 8 * j + L - 1)
                            b = 2 + L % 2
                            q = hQ[:, :].rearrange("p (c b two h) -> p c b two h", c=TT, two=2, h=h)
                            for c in range(TT):
                                mm = pe.matmul(
                                    ps[:, b * HALF + c * 64:b * HALF + (c + 1) * 64],
                                    hK[:, c * P:(c + 1) * P], q[:, c, :, 1, :], start=True, stop=True)
                        mm.then_inc(scores_done, 1)
                    elif at == TURN_AT:
                        pe.wait_ge(scaled, 9 * j + 9)
                        for c in range(TT):
                            mm = pe.transpose(ps[:, c * P:(c + 1) * P], hK[:, c * P:(c + 1) * P], ident[:, :])
                        mm.then_inc(k_turned, 1)
                    elif at == OUTER_AT:
                        pe.wait_ge(k_rows, j + 1)
                        pe.wait_ge(v_loaded, 16 * j + 16)
                        pe.wait_ge(scores_kept, 8 * j + 8)
                        for c in range(TT - 1):
                            mm = pe.matmul(ps[:, 2 * HALF + c * P:2 * HALF + (c + 1) * P],
                                           kS[:, c, :], hV[:, c, :], start=True, stop=True)
                        mm.then_inc(outer_done, 1)
                    elif at == READ_AT:
                        pe.wait_ge(state_step, 7 * j + 7)
                        for c in range(TT):
                            dst = ps[:, c * P:(c + 1) * P]
                            mm = pe.matmul(dst, aT[:, c * P:(c + 1) * P], hV[:, c, :],
                                           start=True, stop=(c == 0))
                            if c:
                                mm = pe.matmul(dst, hQ[:, c * P:(c + 1) * P], st[:, c, :],
                                               start=False, stop=True)
                        mm.then_inc(read_done, 1)
                return hook

            def nothing(at):
                return None

            def last_turns(at):
                if at == 1:
                    turn_tile(R_MIX, TT - 2)
                    turn_tile(R_MIX, TT - 1)

            group(0, 0, True, last_turns)
            group(1, 0, True, nothing)
            group(2, 0, False, nothing)
            pe.nop().then_inc(k_turned, 1)
            pe.nop().then_inc(read_done, 1)
            with pe.Fori(0, HH - 1) as j:
                group(3, j, False, hgrn(j))

            def turn_qk(p, w, b):
                pe.wait_ge(qk_normed, 2 * p + w + 1)
                for t in range(TT):
                    mm = pe.transpose(ps[:, b * HALF + t * P:b * HALF + (t + 1) * P],
                                      (qin, kin)[w][:, t, :], ident[:, :])
                mm.then_inc(qk_turned, 1)

            last_head = hgrn(HH - 1)

            def last_hook(at):
                last_head(at)
                if at == OUTER_AT:
                    pe.wait_ge(proj_evac, 54)
                    turn_qk(0, 0, 4)
                if at == READ_AT:
                    turn_qk(0, 1, 2)
            group(3 + HH - 1, 0, False, last_hook)

            def scores(v):
                p, hd, parts = unit(v)
                if v >= 2:
                    pe.wait_ge(unit_max, v - 1)
                if v % NU == 0:
                    pe.wait_ge(qkT_ready, 2 * p + 2)
                if v == 1:
                    pe.wait_ge(ro_ready, HH + 1)
                rows = slice(hd * DH, (hd + 1) * DH)
                b = score_bank(v) * HALF
                for t, n, c0 in parts:
                    lo = (t - n + 1) * P
                    for c, m in ((c0, min(n * P, HALF - c0)), (HALF, c0 + n * P - HALF)):
                        if c >= c0 and m > 0:
                            mm = pe.matmul(ps[:, b + c:b + c + m], qT[rows, p % 2, t * P:(t + 1) * P],
                                           kT[rows, p % 2, lo + c - c0:lo + c - c0 + m],
                                           start=True, stop=True)
                mm.then_inc(unit_scores, 1)

            def wait_turn_banks(v):
                what = extra(v - 1)
                if v == 1:
                    pe.wait_ge(qkT_ready, 1)
                elif what is None:
                    wait_PT(pe, v - 2)
                elif what[0] == "qk":
                    pe.wait_ge(qkT_ready, 2 * what[1] + what[2] + 1)
                else:
                    pe.wait_ge(head_out, 2 * what[1] + what[2] + 1)

            def turn(v):
                pe.wait_ge(unit_exp, v + 1)
                wait_turn_banks(v + 1)
                for c in range(KEY_TILES):
                    mm = pe.transpose(ps[:, 4 * HALF + c * P:4 * HALF + (c + 1) * P],
                                      Pr[:, v % 2, c * P:(c + 1) * P], ident[:, :])
                mm.then_inc(unit_turned, 1)

            def values(v):
                p, hd, parts = unit(v)
                wait_PT(pe, v)
                if v % NU == 0:
                    pe.wait_ge(av_loaded[p % 2], 16 + 16 * (p // 2))
                if v >= 2:
                    pe.wait_ge(outT_ready, v - 1)
                else:
                    pe.wait_ge(proj_evac, PROJ_OUTS)
                for q, (t, n, c0) in enumerate(parts):
                    b = (6 + v % 2) * HALF + q * P
                    for c in range(n):
                        mm = pe.matmul(ps[:, b:b + P], vin[:, p % 2, t - n + 1 + c, :],
                                       PT[:, v % 2, c0 + c * P:c0 + (c + 1) * P],
                                       start=(c == 0), stop=(c == n - 1))
                mm.then_inc(unit_out, 1)

            def turn_out(p, g):
                pe.wait_ge(outT_ready, NU * p + (NU - 4 if g == 0 else NU))
                for t in range(4):
                    c0 = (4 * (1 - g) + t) * P
                    b = out_bank(p, g) * HALF
                    mm = pe.transpose(ps[:, b + t * P:b + (t + 1) * P],
                                      outT[:, p % 2, c0:c0 + P], ident[:, :])
                mm.then_inc(out_turned, 1)

            for v in range(NV + 3):
                if v < NV:
                    scores(v)
                if 1 <= v <= NV:
                    turn(v - 1)
                if 2 <= v <= NV + 1:
                    values(v - 2)
                what = extra(v)
                if v == NV + 2:
                    turn_tile(R_CAT, 0)
                    turn_tile(R_CAT, 1)
                if what is not None:
                    if v <= NV:
                        wait_PT(pe, v - 1)
                    if what[0] == "qk":
                        turn_qk(what[1], what[2], 4)
                    else:
                        turn_out(what[1], what[2])

            for h in range(2):
                for t in range(TT):
                    d = A_OUT + 8 * h + t
                    if h == 0:
                        pe.wait_ge(hT_ready, TT * R_CAT + t + 1)
                    if h == 0 and t == 1:
                        pe.wait_ge(head_out, 2 * PAIRS)
                    if 8 * h + t >= 4:
                        pe.wait_ge(x_added, d - 3)
                    rows = t if h else CAT_ORDER[t]
                    for k in range(KT):
                        s = (P_OUT + 4 * h + k // 2) % RING
                        if t == 0 and k % 2 == 0:
                            pe.wait_ge(split_lo, P_OUT + 4 * h + k // 2 + 1)
                        c0 = (k % 2) * HALF
                        mm = three(bank(4 + d % 4), [a[:, k, rows * P:(rows + 1) * P] for a in (hThi, hTlo)],
                                   [w[:, s, c0:c0 + HALF] for w in (whi, wlo)], k == 0, k == KT - 1)
                        if t == TT - 1 and k % 2 == 1 and k < KT - 1:
                            mm.then_inc(piece_used, 1)
                    mm.then_inc(row_done, 1)
                    if h == 0 and t + 2 < TT:
                        turn_tile(R_CAT, t + 2)
                    if h == 1 and t >= 1:
                        turn_tile(R_FFN2, t - 1)
            ffn(1, P_FFN2, A_FFN2, R_FFN2)

        @block.scalar
        def _(act):
            def split(n0, adv=0):
                s = n0 % RING
                act.wait_ge(raw_loaded[s], 16 * (n0 // RING + 1) + 4 * adv)
                act.activation(whi[:, s, :], raw[:, s, :], ACT.Copy).then_inc(split_hi, 1)

            def square(R, t):
                q = TT * norm_no(R) + t
                if R == R_FFN1:
                    act.wait_ge(x_loaded[t], 16)
                elif R == R_MIX:
                    act.wait_ge(x_added, A_FFN1 + ADDS_FFN - 16 + 2 * t + 2)
                else:
                    act.wait_ge(x_added, A_OUT + 8 + t + 1)
                if q:
                    act.wait_ge(ss_ready, q)
                if R == R_FFN2 and t == 0:
                    act.wait_ge(qk_ss, 2 * PAIRS)
                act.activation(junk[:, :], xs[:, t, :], ACT.Square,
                               accum_out=ss[:, q:q + 1]).then_inc(ss_ready, 1)

            def hT_hi(R, t):
                r = TT * R + t
                act.wait_ge(turned, r + 1)
                c0 = turn_bank(R, t) * HALF
                if R == R_CAT:
                    if t == 0:
                        act.wait_ge(unit_out, NV)
                    t = CAT_ORDER[t]
                src = ps[:, c0:c0 + D].rearrange("p (k c) -> p k c", k=KT)
                act.activation(hThi[:, :, t * P:(t + 1) * P], src, ACT.Copy).then_inc(hT_hi_ready, 1)

            def used(group, q, advn=0):
                if q < 3:
                    act.wait_ge(piece_used, 3 * group + q + 1 + 3 * advn)
                elif group < 7:
                    act.wait_ge(proj_done, 8 * group + 8 + 8 * advn)
                else:
                    act.wait_ge(row_done, A_OUT + 8 * (group - 7) + 8)

            def ffn(F, base, adds, tail):
                e_base = 2 * FT * F

                def tile(f0, advf, n0, adv):
                    for h in range(2):
                        e = e_base + 2 * f0 + h
                        act.wait_ge(gate_done, e + 1 + 2 * advf)
                        if e >= 2:
                            act.wait_ge(prod_done, e - 1 + 2 * advf)
                        act.activation(sil[:, h, :], bank(h), ACT.Silu).then_inc(silu_done, 1)
                        if h == 0:
                            split(n0 + 2, adv)
                    split(n0 + 3, adv)
                    for h in range(2):
                        e = e_base + 2 * f0 + h
                        act.wait_ge(prod_done, e + 1 + 2 * advf)
                        act.activation(hidhi[:, (f0 // 2) % 2, f0 % 2, h * HALF:(h + 1) * HALF],
                                       prod[:, h, :], ACT.Copy).then_inc(hid_hi_ready, 1)

                tile(0, 0, base, 0)
                tile(1, 0, base + 2, 0)
                with act.Fori(0, NG // 2) as i:
                    for g in range(2):
                        n0 = base + 4 + 6 * g
                        tile(2 + 2 * g, 4 * i, n0, 12 * i)
                        tile(3 + 2 * g, 4 * i, n0 + 2, 12 * i)
                        last = g == 1
                        split(n0 + 6, 12 * i)
                        split(n0 + 7, 12 * i)
                if tail:
                    act.wait_ge(row_done, adds + 16 * (NG - 1))
                    split(base + PIECES_FFN)
                    split(base + PIECES_FFN + 1)
                    for t in range(TT + 2):
                        if t >= 2:
                            hT_hi(R_MIX, t - 2)
                        if t < TT:
                            square(R_MIX, t)
                        if t == TT - 1:
                            act.wait_ge(row_done, A_OUT)
                            split(P_MIX + 2)
                            split(P_MIX + 3)

            act.dma_start(ident[:, :], identity).then_inc(ident_loaded, 16)
            for t in range(4):
                square(R_FFN1, t)
            for t in range(3):
                hT_hi(R_FFN1, t)
            split(0)
            hT_hi(R_FFN1, 3)
            split(1)
            for t in range(4, TT):
                square(R_FFN1, t)
            for t in range(4, TT):
                hT_hi(R_FFN1, t)
            ffn(0, P_FFN1, A_FFN1, True)

            def stage(o):
                return y[:, 0, (o % 2) * HALF:(o % 2 + 1) * HALF]

            def evac(n0, advn, o, func):
                idx = 8 * n0 + o
                act.wait_ge(proj_done, idx + 1 + 8 * advn)
                if idx >= 2:
                    act.wait_ge(proj_stored[o % 2], 16 * (idx // 2) + 64 * advn)
                if func == ACT.Sigmoid:
                    act.activation(stage(o), bank(4 + o % 4), ACT.Sigmoid).then_inc(sig_ready, 1)
                    act.wait_ge(sig_ready, o + 1)
                    f = FEATURE_ORDER[o][0]
                    act.activation(stage(o), stage(o), ACT.Identity, scale=lb[:, 1, f:f + 1],
                                   bias=lb[:, 0, f:f + 1]).then_inc(proj_evac, 1)
                else:
                    act.activation(stage(o), bank(4 + o % 4), func).then_inc(proj_evac, 1)

            def store(n0, advn, o, feature):
                idx = 8 * n0 + o
                act.wait_ge(proj_evac, idx + 1 + 8 * advn)
                if feature:
                    f, h = FEATURE_ORDER[o]
                    row = n0 * HALF + f * P
                    dst = feat[row:row + P, h * HALF:(h + 1) * HALF]
                else:
                    dst = tok[o * P:(o + 1) * P, ds(n0 - 2 + advn, 1), :].rearrange("p a c -> p (a c)")
                act.dma_start(dst, stage(o)).then_inc(proj_stored[o % 2], 16)

            def group(n0, advn, func, feature=False, head=None, first_head=False, square_at=()):
                for o in range(7):
                    evac(n0, advn, o, func)
                    store(n0, advn, o, feature)
                    if o in square_at:
                        square_qk(0, square_at.index(o))
                if head is not None:
                    if not first_head:
                        act.wait_ge(ro_gated, head)
                    act.wait_ge(k_turned, head + 2)
                    act.activation(kS[:, :, :].rearrange("p a b -> p (a b)"), ps[:, 0:1024], ACT.Copy)\
                       .then_inc(k_rows, 1)
                for q in range(4):
                    used(n0, q, advn)
                    split(P_MIX + 4 * n0 + 4 + q, 4 * advn)
                evac(n0, advn, 7, func)
                store(n0, advn, 7, feature)
                if head is not None:
                    act.wait_ge(read_done, head + 2)
                    act.wait_ge(read_ss, head + 1)
                    if square_at:
                        act.wait_ge(qk_ss, 2)
                    act.wait_ge(ss_ready, 2 * TT)
                    act.activation(junk[:, :], ps[:, 0:1024], ACT.Square).then_inc(read_sq, 1)

            def square_qk(p, w):
                act.wait_ge(qk_loaded[w], 16 * p + 16)
                if p == 0 and w == 0:
                    act.wait_ge(read_ss, HH)
                else:
                    act.wait_ge(qk_ss, 2 * p + w)
                act.activation(junk[:, :], (qin, kin)[w].rearrange("p a b -> p (a b)"),
                               ACT.Square).then_inc(qk_sq, 1)

            group(0, 0, ACT.Silu, True)
            act.wait_ge(lb_diff, 1)
            act.activation(lb[:, 0, :], lb[:, 2, :], ACT.Sigmoid).then_inc(lb_sig, 1)
            act.wait_ge(lb_ready, 1)
            group(1, 0, ACT.Sigmoid, True)
            group(2, 0, ACT.Copy)
            group(3, 0, ACT.Silu, head=0, first_head=True)
            with act.Fori(1, HH - 1) as j:
                group(3, j, ACT.Copy, head=j)
            group(3 + HH - 1, 0, ACT.Copy, head=HH - 1, square_at=(2, 4))

            def take_qk(p, w, b):
                act.wait_ge(qk_turned, 2 * p + w + 1)
                act.activation((qT, kT)[w][:, p % 2, :], ps[:, b * HALF:b * HALF + T], ACT.Copy,
                               scale=qkg[:, w:w + 1]).then_inc(qkT_ready, 1)

            def keep_out(v):
                p, hd, parts = unit(v)
                act.wait_ge(unit_out, v + 1)
                if p >= 2 and v % NU < 2:
                    act.wait_ge(out_turned, 2 * (p - 2) + 2)
                rows = slice(hd * DH, (hd + 1) * DH)
                for q, (t, n, c0) in enumerate(parts):
                    b = (6 + v % 2) * HALF + q * P
                    last = act.activation(outT[rows, p % 2, t * P:(t + 1) * P], ps[rows, b:b + P], ACT.Copy)
                last.then_inc(outT_ready, 1)

            act.wait_ge(proj_done, PROJ_OUTS)
            act.wait_ge(qk_gain_ready, 1)
            take_qk(0, 0, 4)
            take_qk(0, 1, 2)
            for v in range(NV + 2):
                if v < NV:
                    p, hd, parts = unit(v)
                    act.wait_ge(unit_max, v + 1)
                    if v >= 2:
                        act.wait_ge(unit_turned, v - 1)
                    if p >= 2 and v % NU == 0:
                        act.wait_ge(rcp_ready, 2 * (p - 2) + 2)
                    for t, n, c0 in parts:
                        last = act.activation(Pr[:, v % 2, c0:c0 + n * P], S[:, v % 2, c0:c0 + n * P],
                                              ACT.Exp, scale=-1.0, bias=nmax[:, hd, t:t + 1],
                                              accum_out=psumr[:, p % 2, hd, t:t + 1])
                    last.then_inc(unit_exp, 1)
                if 1 <= v <= NV and by_scalar(v - 1):
                    act.wait_ge(unit_turned, v)
                    if v >= 3:
                        act.wait_ge(unit_out, v - 2)
                    act.activation(PT[:, (v - 1) % 2, :], ps[:, 4 * HALF:4 * HALF + BAND], ACT.Copy)\
                       .then_inc(PT_by_scalar, 1)
                if v >= 2:
                    keep_out(v - 2)
                if v < NV - NU and v % NU in SQUARE_AT:
                    square_qk(v // NU + 1, SQUARE_AT.index(v % NU))
                what = extra(v)
                if what is not None and what[0] == "qk":
                    take_qk(what[1], what[2], 4)

            for t in range(TT):
                hT_hi(R_CAT, t)
            for q in range(4):
                used(7, q)
                split(P_OUT + 4 + q)
            for t in range(TT + 1):
                if t == TT - 1:
                    for q in range(2):
                        used(8, q)
                        split(P_FFN2 + q)
                if t < TT:
                    square(R_FFN2, t)
                if t >= 1:
                    hT_hi(R_FFN2, t - 1)
            ffn(1, P_FFN2, A_FFN2, False)
            for t in range(TT):
                act.wait_ge(x_added, A_FFN2 + ADDS_FFN - 16 + 2 * t + 2)
                act.dma_start(out[0, t * P:(t + 1) * P, :], xs[:, t, :]).then_inc(out_stored, 16)
            act.wait_ge(out_stored, 16 * TT)

        @block.vector
        def _(dve):
            def split(n0, adv=0):
                s = n0 % RING
                dve.wait_ge(split_hi, n0 + 1 + adv)
                dve.tensor_tensor(wlo[:, s, :], raw[:, s, :], whi[:, s, :].bitcast(F32), ALU.subtract)\
                   .then_inc(split_lo, 1)

            def normalise(R, t):
                q = TT * norm_no(R) + t
                dve.wait_ge(rstd_ready, q + 1)
                if t == 0:
                    dve.wait_ge(gain_loaded, 16 * norm_no(R) + 16)
                if t >= 2 and R != R_FFN1:
                    dve.wait_ge(turned, TT * R + t - 1)
                dve.scalar_tensor_tensor(y_slot(R, t), xs[:, t, :], rstd[:, q:q + 1], gain[:, :],
                                         ALU.mult, ALU.mult).then_inc(y_ready, 1)

            def hT_lo(R, t):
                r = TT * R + t
                dve.wait_ge(hT_hi_ready, r + 1)
                c0 = turn_bank(R, t) * HALF
                if R == R_CAT:
                    t = CAT_ORDER[t]
                src = ps[:, c0:c0 + D].rearrange("p (k c) -> p k c", k=KT)
                dve.tensor_tensor(hTlo[:, :, t * P:(t + 1) * P], src,
                                  hThi[:, :, t * P:(t + 1) * P].bitcast(F32), ALU.subtract)\
                   .then_inc(hT_ready, 1)

            def add(d0, advd, t, h, scale):
                dve.wait_ge(row_done, d0 + 1 + advd)
                dst = xs[:, t, h * HALF:(h + 1) * HALF]
                dve.scalar_tensor_tensor(dst, bank(4 + d0 % 4), scale, dst, ALU.mult, ALU.add)\
                   .then_inc(x_added, 1)

            def ffn(F, base, adds, tail):
                e_base = 2 * FT * F

                def tile(f0, advf, n0, adv):
                    split(n0 + 2, adv)
                    split(n0 + 3, adv)
                    for h in range(2):
                        e = e_base + 2 * f0 + h
                        dve.wait_ge(silu_done, e + 1 + 2 * advf)
                        dve.wait_ge(up_done, e + 1 + 2 * advf)
                        if e >= 2:
                            dve.wait_ge(hid_ready, e - 1 + 2 * advf)
                        dve.tensor_tensor(prod[:, h, :], bank(2 + h), sil[:, h, :], ALU.mult)\
                           .then_inc(prod_done, 1)
                    for h in range(2):
                        e = e_base + 2 * f0 + h
                        dve.wait_ge(hid_hi_ready, e + 1 + 2 * advf)
                        at = (slice(None), (f0 // 2) % 2, f0 % 2, slice(h * HALF, (h + 1) * HALF))
                        dve.tensor_tensor(hidlo[at], prod[:, h, :], hidhi[at].bitcast(F32), ALU.subtract)\
                           .then_inc(hid_ready, 1)

                tile(0, 0, base, 0)
                tile(1, 0, base + 2, 0)
                with dve.Fori(0, NG // 2) as i:
                    for g in range(2):
                        n0 = base + 4 + 6 * g
                        tile(2 + 2 * g, 4 * i, n0, 12 * i)
                        tile(3 + 2 * g, 4 * i, n0 + 2, 12 * i)
                        for t in range(TT):
                            for h in range(2):
                                add(adds + 16 * g + 2 * t + h, 32 * i, t, h, 0.5)
                            if t in (1, 3):
                                split(n0 + 6 + t // 2, 12 * i)
                d0 = adds + 16 * (NG - 1)
                if tail:
                    split(base + PIECES_FFN)
                    split(base + PIECES_FFN + 1)
                for t in range(TT):
                    for h in range(2):
                        add(d0 + 2 * t + h, 0, t, h, 0.5)
                    if tail:
                        if t >= 1:
                            normalise(R_MIX, t - 1)
                        if t >= 2:
                            hT_lo(R_MIX, t - 2)
                if tail:
                    split(P_MIX + 2)
                    split(P_MIX + 3)
                    normalise(R_MIX, TT - 1)
                    hT_lo(R_MIX, TT - 2)
                    hT_lo(R_MIX, TT - 1)

            for t in range(4):
                normalise(R_FFN1, t)
            for t in range(3):
                hT_lo(R_FFN1, t)
            split(0)
            hT_lo(R_FFN1, 3)
            split(1)
            for t in range(4, TT):
                normalise(R_FFN1, t)
            for t in range(4, TT):
                hT_lo(R_FFN1, t)
            ffn(0, P_FFN1, A_FFN1, True)

            dve.wait_ge(lb_loaded, 16)
            dve.tensor_tensor(lb[:, 2, :], lbs[:, 0, :], lbs[:, 1, :], ALU.subtract).then_inc(lb_diff, 1)
            dve.wait_ge(mask_loaded, 16)
            for L in range(LEVELS - 1):
                m = bass.AP(tot, L * 64, [list(tot[:, :].ap[0]), [0, TT], [1, 64]])
                dve.tensor_copy(mk[:, L * HALF:(L + 1) * HALF].rearrange("p (c t) -> p c t", c=TT), m)\
                   .then_inc(mask_set, 1)
            dve.wait_ge(rel_loaded, 16)
            n_far = EXT - 1 - (REL_CLIP + 127)
            dve.tensor_copy(extrow[:, n_far:EXT - 1], relrow[:, N_REL - 2:0:-1]).then_inc(ext_step, 1)
            dve.tensor_copy(extrow[:, 0:n_far], relrow[:, N_REL - 1:N_REL].to_broadcast([AH, n_far]))\
               .then_inc(ext_step, 1)
            dve.memset(extrow[:, EXT - 1:EXT], 0.0).then_inc(ext_step, 1)
            dve.wait_ge(qk_gain_loaded, 64)
            dve.tensor_scalar(qkg[:, 0:1], qkg[:, 0:1], DH ** -0.5, None, ALU.mult).then_inc(qk_gain_ready, 1)
            for q in range(4):
                split(P_MIX + 4 + q)
            dve.wait_ge(lb_sig, 1)
            dve.tensor_scalar(lb[:, 1, :], lb[:, 0, :], -1.0, 1.0, ALU.mult, ALU.add).then_inc(lb_ready, 1)
            for n in (1, 2):
                for q in range(4):
                    split(P_MIX + 4 * n + 4 + q)

            def head(j, prepare=None):
                n = [0]

                def link(ins):
                    n[0] += 1
                    ins.then_inc(hgrn_step, 1)
                    dve.wait_ge(hgrn_step, n[0] + per_head * j)

                def keep_scores(L):
                    if L:
                        dve.wait_ge(mask_set, LEVELS - 1)
                    dve.wait_ge(scores_done, 8 * j + L + 1)
                    if L == 0:
                        dst = aT[:, :].rearrange("p (c t) -> p c t", c=TT)
                        src = ps[:, 0:1024].rearrange("p (c t) -> p c t", c=TT)
                        eye = bass.AP(ident, 0, [list(ident[:, :].ap[0]), [0, TT], [1, P]])
                        dve.tensor_tensor(dst, src, eye, ALU.mult).then_inc(scores_kept, 1)
                        return
                    dve.wait_ge(scores_kept, 8 * j + L)
                    h = 1 << (L - 1)
                    dst = aT[:, :].rearrange("p (b two h) -> p b two h", two=2, h=h)[:, :, 1, :]
                    src = bank(2 + L % 2).rearrange("p (b h) -> p b h", h=h)
                    m = mk[:, (L - 1) * HALF:L * HALF].rearrange("p (b h) -> p b h", h=h)
                    dve.copy_predicated(dst, m, src).then_inc(scores_kept, 1)

                dve.wait_ge(fq_loaded, 32 * j + 32)
                dve.wait_ge(k_turned, j + 1)
                dve.tensor_scalar(hK[:, :], fF[:, :], -1.0, 1.0, ALU.mult, ALU.add).then_inc(scaled, 1)
                dve.wait_ge(read_done, j + 1)
                link(dve.tensor_tensor(hQ[:, :], fQ[:, :], fF[:, :], ALU.mult))
                dve.wait_ge(scaled, 9 * j + 1)
                dve.nop().then_inc(scaled, 1)
                keep_scores(0)
                before, size = fF[:, :], T
                used = 0
                for L in range(2, LEVELS + 1):
                    s = 1 << (L - 2)
                    tt = before.rearrange("p (b two) -> p b two", two=2)
                    kk = hK[:, :].rearrange("p (b two s) -> p b two s", two=2, s=s)
                    qq = hQ[:, :].rearrange("p (b two s) -> p b two s", two=2, s=s)
                    nb = T // (2 * s)
                    after = tot[:, used:used + nb]
                    used += nb
                    dve.wait_ge(scores_done, 8 * j + L)
                    link(dve.tensor_tensor(kk[:, :, 0, :], kk[:, :, 0, :],
                                           tt[:, :, 1:2].to_broadcast([P, nb, s]), ALU.mult))
                    link(dve.tensor_tensor(qq[:, :, 1, :], qq[:, :, 1, :],
                                           tt[:, :, 0:1].to_broadcast([P, nb, s]), ALU.mult))
                    link(dve.tensor_tensor(after, tt[:, :, 0], tt[:, :, 1], ALU.mult))
                    dve.nop().then_inc(scaled, 1)
                    keep_scores(L - 1)
                    before = after
                    if prepare and L >= 5:
                        prepare[L - 5]()
                dve.wait_ge(outer_done, j + 1)
                for c in range(TT - 1):
                    kv = ps[:, 2 * HALF + c * P:2 * HALF + (c + 1) * P]
                    if c == 0:
                        dve.tensor_copy(st[:, 1, :], kv).then_inc(state_step, 1)
                    else:
                        dve.wait_ge(state_step, 7 * j + c)
                        dve.scalar_tensor_tensor(st[:, c + 1, :], st[:, c, :], before[:, c:c + 1], kv,
                                                 ALU.mult, ALU.add).then_inc(state_step, 1)
                for q in range(4):
                    split(P_MIX + 16 + q, 4 * j)
                dve.wait_ge(read_sq, j + 1)
                dve.tensor_reduce(sso[:, :], junk[:, :].rearrange("p (c v) -> p c v", c=TT), AX_X,
                                  ALU.add).then_inc(read_ss, 1)
                dve.wait_ge(read_rstd, j + 1)
                dve.tensor_tensor(kS[:, :, :], ps[:, 0:1024].rearrange("p (c v) -> p c v", c=TT),
                                  rso[:, :].unsqueeze(2).to_broadcast([P, TT, P]), ALU.mult)\
                   .then_inc(ro_ready, 1)

            per_head = 1 + 3 * 7
            dve.wait_ge(ext_stored, 16)
            dve.nop().then_inc(read_ss, 1)
            dve.nop().then_inc(ro_ready, 1)
            with dve.Fori(0, HH - 1) as j:
                head(j)

            def sum_qk(p, w):
                dve.wait_ge(qk_sq, 2 * p + w + 1)
                dve.tensor_reduce(ssq[:, w, :], junk[:, :].rearrange("p (g d) -> p g d", d=DH), AX_X,
                                  ALU.add).then_inc(qk_ss, 1)

            def norm_qk(p, w):
                dve.wait_ge(qk_rstd, 2 * p + w + 1)
                v = (qin, kin)[w].rearrange("p t (h d) -> p (t h) d", d=DH)
                r = rsq[:, w, :].unsqueeze(2).to_broadcast([P, 16, DH])
                dve.tensor_tensor(v, v, r, ALU.mult).then_inc(qk_normed, 1)

            head(HH - 1, [lambda: sum_qk(0, 0), lambda: norm_qk(0, 0), lambda: sum_qk(0, 1),
                          lambda: norm_qk(0, 1)])

            def head_output(p, g):
                tiles = slice(4 * (1 - g), 4 * (1 - g) + 4)
                dve.wait_ge(unit_exp, NU * p + (NU if g else NU - 4))
                dve.reciprocal(rcp[:, p % 2, :, tiles], psumr[:, p % 2, :, tiles]).then_inc(rcp_ready, 1)
                dve.wait_ge(rcp_ready, 2 * p + g + 1)
                dve.wait_ge(out_turned, 2 * p + g + 1)
                r = rcp[:, p % 2, :, tiles].rearrange("p h t -> p t h").unsqueeze(3).to_broadcast([P, 4, 2, DH])
                dve.tensor_tensor(cat[:, tiles, p * P:(p + 1) * P].rearrange("p t (h d) -> p t h d", d=DH),
                                  bank(out_bank(p, g)).rearrange("p (t h d) -> p t h d", t=4, d=DH), r, ALU.mult)\
                   .then_inc(head_out, 1)

            dve.wait_ge(proj_done, PROJ_OUTS)
            for v in range(NV + 3):
                if v < NV:
                    p, hd, parts = unit(v)
                    dve.wait_ge(unit_scores, v + 1)
                    if v % NU == 0:
                        dve.wait_ge(bias_masked, 4 * p + 4)
                    if v >= 2:
                        dve.wait_ge(unit_exp, v - 1)
                    for t, n, c0 in parts:
                        b = score_bank(v) * HALF
                        last = dve.tensor_tensor_reduce(
                            S[:, v % 2, c0:c0 + n * P], ps[:, b + c0:b + c0 + n * P],
                            bias[:, p % 2, hd, BAND - n * P:BAND], -1.0, 3.0e38, ALU.add, ALU.min,
                            nmax[:, hd, t:t + 1])
                    last.then_inc(unit_max, 1)
                if 1 <= v <= NV and not by_scalar(v - 1):
                    dve.wait_ge(unit_turned, v)
                    if v >= 3:
                        dve.wait_ge(unit_out, v - 2)
                    dve.tensor_copy(PT[:, (v - 1) % 2, :], ps[:, 4 * HALF:4 * HALF + BAND])\
                       .then_inc(PT_by_vector, 1)
                if v < NV - NU:
                    if v % NU in SUM_AT:
                        sum_qk(v // NU + 1, SUM_AT.index(v % NU))
                    if v % NU in NORM_AT:
                        norm_qk(v // NU + 1, NORM_AT.index(v % NU))
                what = extra(v)
                if what is not None and what[0] == "out":
                    if what[1] == 0 and what[2] == 0:
                        dve.wait_ge(ro_stored, 16 * HH)
                    if v == NV + 2:
                        hT_lo(R_CAT, 0)
                    head_output(what[1], what[2])

            hT_lo(R_CAT, 1)
            for t in range(TT):
                if t == TT - 1:
                    for q in range(4):
                        split(P_OUT + 4 + q)
                add(A_OUT + t, 0, CAT_ORDER[t], 0, 1.0)
                if t + 2 < TT:
                    hT_lo(R_CAT, t + 2)
            for t in range(TT):
                if t == TT - 1:
                    split(P_FFN2)
                    split(P_FFN2 + 1)
                add(A_OUT + 8 + t, 0, t, 1, 1.0)
                if t >= 1:
                    hT_lo(R_FFN2, t - 1)
                normalise(R_FFN2, t)
            hT_lo(R_FFN2, TT - 1)
            ffn(1, P_FFN2, A_FFN2, False)

        @block.gpsimd
        def _(pool):
            pool.memset(mhalf[:, :], -0.5).then_inc(mhalf_set, 1)
            pool.dma_start(gain[:, :], ffn1_norm_g[0:1, :].to_broadcast([P, D])).then_inc(gain_loaded, 16)
            pool.wait_ge(mhalf_set, 1)

            def rms(R):
                for t in range(TT):
                    q = TT * norm_no(R) + t
                    pool.wait_ge(ss_ready, q + 1)
                    pool.tensor_scalar(rstd[:, q:q + 1], ss[:, q:q + 1], 1.0 / D, EPS, ALU.mult, ALU.add)\
                        .then_inc(var_ready, 1)
                    pool.wait_ge(var_ready, q + 1)
                    pool.tensor_tensor(rstd[:, q:q + 1], rstd[:, q:q + 1], mhalf[:, 0:1], ALU.pow)\
                        .then_inc(rstd_ready, 1)

            rms(R_FFN1)
            pool.dma_start(lbs[:, :, :], hgrn_lower_bounds.rearrange("r (h p) -> p r h", p=P),
                           allow_slow_non_contiguous=True).then_inc(lb_loaded, 16)
            pool.dma_start(gn[:, :], hgrn_out_norm_g[0:1, :].to_broadcast([P, P])).then_inc(gn_loaded, 16)
            pool.dma_start(qkg[0:DH, 0:1], attn_q_norm_g.rearrange("a d -> d a"),
                           allow_slow_non_contiguous=True).then_inc(qk_gain_loaded, 16)
            pool.dma_start(qkg[DH:P, 0:1], attn_q_norm_g.rearrange("a d -> d a"),
                           allow_slow_non_contiguous=True).then_inc(qk_gain_loaded, 16)
            pool.dma_start(qkg[0:DH, 1:2], attn_k_norm_g.rearrange("a d -> d a"),
                           allow_slow_non_contiguous=True).then_inc(qk_gain_loaded, 16)
            pool.dma_start(qkg[DH:P, 1:2], attn_k_norm_g.rearrange("a d -> d a"),
                           allow_slow_non_contiguous=True).then_inc(qk_gain_loaded, 16)
            pool.wait_ge(y_ready, TT)
            pool.dma_start(gain[:, :], mix_norm_g[0:1, :].to_broadcast([P, D])).then_inc(gain_loaded, 16)
            rms(R_MIX)

            def stored(n):
                for s in range(2):
                    pool.wait_ge(proj_stored[s], 64 * n)

            def load_fq(j):
                pool.dma_start(fF[:, :], feat[ds(j * P + HALF, P), :]).then_inc(fq_loaded, 16)
                pool.dma_start(fQ[:, :], feat[ds(j * P, P), :]).then_inc(fq_loaded, 16)

            def load_v(j):
                pool.dma_start(hV[:, :, :], tok[:, 0, ds(j * P, P)].rearrange("(t p) c -> p t c", p=P))\
                    .then_inc(v_loaded, 16)

            def load_g(j):
                pool.dma_start(hG[:, :, :], tok[:, 1, ds(j * P, P)].rearrange("(t p) c -> p t c", p=P))\
                    .then_inc(g_loaded, 16)

            def read_rms(j):
                pool.wait_ge(read_ss, j + 2)
                pool.nop().then_inc(pool_passed, 1)
                pool.tensor_scalar(rso[:, :], sso[:, :], 1.0 / P, EPS, ALU.mult, ALU.add).then_inc(read_var, 1)
                pool.wait_ge(read_var, j + 1)
                pool.tensor_tensor(rso[:, :], rso[:, :], mhalf[:, 0:TT], ALU.pow).then_inc(read_rstd, 1)

            def finish(j):
                pool.wait_ge(gn_loaded, 16)
                pool.wait_ge(g_loaded, 16 * j + 16)
                gb = bass.AP(gn, 0, [list(gn[:, :].ap[0]), [0, TT], [1, P]])
                pool.tensor_tensor(hG[:, :, :], hG[:, :, :], gb, ALU.mult).then_inc(gate_gained, 1)
                pool.wait_ge(ro_ready, j + 2)
                pool.wait_ge(gate_gained, j + 1)
                pool.tensor_tensor(hG[:, :, :], hG[:, :, :], kS[:, :, :], ALU.mult).then_inc(ro_gated, 1)
                pool.wait_ge(ro_gated, j + 1)
                pool.dma_start(ro_d[:, ds(j * P, P)].rearrange("(t p) c -> p t c", p=P), hG[:, :, :])\
                    .then_inc(ro_stored, 16)

            pool.wait_ge(x_added, A_OUT)
            pool.dma_start(tot[:, 0:(LEVELS - 1) * 64], masks).then_inc(mask_loaded, 16)
            pool.dma_start(relrow, attn_rel_bias[0]).then_inc(rel_loaded, 16)
            pool.wait_ge(ext_step, 3)
            pool.dma_start(ext_d, extrow).then_inc(ext_stored, 16)
            pool.wait_ge(ext_stored, 16)
            skew = bass.AP(ext_d.tensor, P - 1, [[EXT, AH], [-1, P], [1, BAND]])
            pool.dma_start(bias_d, skew).then_inc(bias_stored, 16)
            stored(2)
            load_fq(0)
            stored(3)
            load_v(0)
            with pool.Fori(0, HH - 1) as j:
                pool.wait_ge(scores_done, 8 * j + 1)
                pool.wait_ge(scaled, 9 * j + 3)
                load_fq(j + 1)
                read_rms(j)
                stored(4)
                load_g(j)
                pool.wait_ge(read_done, j + 2)
                load_v(j + 1)
                finish(j)
                pool.wait_ge(ro_stored, 16 * j + 16)

            def load_qk(p):
                for w in range(2):
                    pool.dma_start((qin, kin)[w], tok[:, 2 + w, p * P:(p + 1) * P]
                                   .rearrange("(t p) c -> p t c", p=P)).then_inc(qk_loaded[w], 16)

            def load_bias(p):
                pool.dma_start(bias[:, p % 2, :, :], bias_d[2 * p:2 * p + 2].rearrange("h t s -> t h s"))\
                    .then_inc(bias_loaded, 16)

            def load_v(p):
                pool.dma_start(vin[:, p % 2, :, :], tok[:, 4, p * P:(p + 1) * P]
                               .rearrange("(t p) c -> p t c", p=P)).then_inc(av_loaded[p % 2], 16)

            def mask_bias(p):
                pool.wait_ge(bias_loaded, 16 * p + 16)
                for hd in range(2):
                    pool.memset(bias[CHUNK:P, p % 2, hd, 0:CHUNK], MASKED).then_inc(bias_masked, 1)
                    pool.memset(bias[0:CHUNK, p % 2, hd, BAND - CHUNK:BAND], MASKED).then_inc(bias_masked, 1)
                pool.wait_ge(bias_masked, 4 * p + 4)

            def qk_rms(p):
                for w in range(2):
                    n = 2 * p + w
                    pool.wait_ge(qk_ss, n + 1)
                    pool.tensor_scalar(rsq[:, w, :], ssq[:, w, :], 1.0 / DH, EPS, ALU.mult, ALU.add)\
                        .then_inc(qk_var, 1)
                    pool.wait_ge(qk_var, n + 1)
                    pool.tensor_tensor(rsq[:, w, :], rsq[:, w, :], mhalf[:, 0:16], ALU.pow).then_inc(qk_rstd, 1)

            stored(6)
            pool.wait_ge(y_ready, 2 * TT)
            pool.wait_ge(turned, 2 * TT)
            load_qk(0)
            load_g(HH - 1)
            qk_rms(0)
            pool.wait_ge(bias_stored, 16)
            pool.wait_ge(proj_done, PROJ_OUTS)
            load_bias(0)
            read_rms(HH - 1)
            stored(7)
            load_v(0)
            pool.wait_ge(read_rstd, HH)
            mask_bias(0)
            finish(HH - 1)
            for p in range(1, PAIRS):
                pool.wait_ge(qk_turned, 2 * p)
                load_qk(p)
                if p >= 2:
                    pool.wait_ge(unit_out, NU * (p - 1))
                load_bias(p)
                load_v(p)
                mask_bias(p)
                if p == 1:
                    pool.wait_ge(ro_stored, 16 * HH)
                    pool.dma_start(cat[:, :, HALF:D], ro_d.rearrange("(t p) c -> p t c", p=P))\
                        .then_inc(cat_loaded, 16)
                qk_rms(p)
            pool.wait_ge(qk_turned, 2 * PAIRS)
            pool.dma_start(gain[:, :], ffn2_norm_g[0:1, :].to_broadcast([P, D])).then_inc(gain_loaded, 16)
            rms(R_FFN2)


_NAMES = ["x", "ffn1_norm_g", "ffn1_w_gate", "ffn1_w_up", "ffn1_w_down", "mix_norm_g", "w_in",
          "attn_q_norm_g", "attn_k_norm_g", "attn_rel_bias", "hgrn_lower_bounds", "hgrn_out_norm_g",
          "w_out", "ffn2_norm_g", "ffn2_w_gate", "ffn2_w_up", "ffn2_w_down"]


def kernel(**inputs):
    import concourse.bacc as bacc
    from concourse.bass_utils import run_bass_kernel_spmd

    nc = bacc.Bacc("TRN2", target_bir_lowering=False, num_devices=1)
    arrays = {n: np.ascontiguousarray(inputs[n]) for n in _NAMES}
    arrays["identity"] = np.eye(P, dtype=np.float32)
    arrays["masks"] = level_masks()
    args = [nc.dram_tensor(n, a.shape, mybir.dt.from_np(a.dtype), kind="ExternalInput").ap()
            for n, a in arrays.items()]
    out = nc.dram_tensor("out", (1, T, D), F32, kind="ExternalOutput").ap()
    build(nc, *args, out)
    r = run_bass_kernel_spmd(nc, [arrays], core_ids=[0])
    return r.results[0]["out"]
```
